# Optimizing a Trainium2 kernel written in Bass

```python
import math
import jax, jax.numpy as jnp
from jax import lax
import numpy as np

D_MODEL = 1024
BATCH = 1
SEQ = 256
DEPTH = 1
DEC_BATCH = 8
DEC_SEQ = 1
PAST_LEN = 2048
PAGE_SIZE = 128

N_HEADS = 16
QK_NOPE = 64
QK_ROPE = 32
QK_DIM = QK_NOPE + QK_ROPE
V_HEAD = 64
Q_LORA = 384
KV_LORA = 256
ROPE_THETA = 10000.0
CONV_CH = 1024
CONV_WIDTH = 31
CONV_BUF = CONV_WIDTH - 1
D_FF = 2816
N_BRANCH = 2
N_MOD = 9
Q_BLOCK = 128
EPS = 1e-6
IN_COLS = Q_LORA + KV_LORA + QK_ROPE + 2 * CONV_CH + N_BRANCH * D_MODEL

kernel_name = 'hybrid_mla_conformer_conv_macaron_step'

def _rmsnorm(x, g):
    xf = x.astype(jnp.float32)
    y = xf * lax.rsqrt(jnp.mean(xf * xf, axis=-1, keepdims=True) + EPS)
    return (y * g.astype(jnp.float32)).astype(x.dtype)

def _layernorm(x, g, b):
    xf = x.astype(jnp.float32)
    mu = jnp.mean(xf, axis=-1, keepdims=True)
    var = jnp.mean(jnp.square(xf - mu), axis=-1, keepdims=True)
    y = (xf - mu) * lax.rsqrt(var + EPS)
    return (y * g.astype(jnp.float32) + b.astype(jnp.float32)).astype(x.dtype)

def _modulate(xn, shift, scale):
    return xn * (1 + scale) + shift

def _swiglu(x, w_in, w_out):
    up, gt = jnp.split(x @ w_in, 2, axis=-1)
    return (jax.nn.silu(gt) * up) @ w_out

def _adaln(c, w_ada, b_ada):
    mod = jax.nn.silu(c) @ w_ada + b_ada
    return jnp.split(mod[:, None, :], N_MOD, axis=-1)

def _rope(x, pos):
    half = x.shape[-1] // 2
    inv = ROPE_THETA ** (-jnp.arange(half, dtype=jnp.float32) / half)
    ang = pos.astype(jnp.float32)[:, None] * inv[None, :]
    cos = jnp.cos(ang)[:, None, :]
    sin = jnp.sin(ang)[:, None, :]
    xf = x.astype(jnp.float32)
    x1, x2 = xf[..., :half], xf[..., half:]
    out = jnp.concatenate([x1 * cos - x2 * sin, x1 * sin + x2 * cos], axis=-1)
    return out.astype(x.dtype)

def _split_in(p):
    cuts = [Q_LORA, Q_LORA + KV_LORA, Q_LORA + KV_LORA + QK_ROPE,
            Q_LORA + KV_LORA + QK_ROPE + 2 * CONV_CH]
    return jnp.split(p, cuts, axis=-1)

def _mla_query(q_a, pos, g_q_lat, w_uq, g_q_head):
    q = jnp.einsum('btr,rhd->bthd', _rmsnorm(q_a, g_q_lat), w_uq)
    q = jnp.concatenate([q[..., :QK_NOPE], _rope(q[..., QK_NOPE:], pos)], axis=-1)
    return _rmsnorm(q, g_q_head)

def _mla_latent(kv_a, k_pe, pos, g_kv_lat):
    return _rmsnorm(kv_a, g_kv_lat), _rope(k_pe[:, :, None, :], pos)[:, :, 0, :]

def _mla_keys(kv_lat, k_rope, w_uk, g_k_head):
    k_nope = jnp.einsum('btl,lhd->bthd', kv_lat, w_uk)
    k_r = jnp.broadcast_to(k_rope[:, :, None, :], k_nope.shape[:-1] + (QK_ROPE,)).astype(k_nope.dtype)
    return _rmsnorm(jnp.concatenate([k_nope, k_r], axis=-1), g_k_head)

def _attn_prompt(q, kv_lat, k_rope, w_uk, w_uv, g_k_head):
    b, t = q.shape[0], q.shape[1]
    k = _mla_keys(kv_lat, k_rope, w_uk, g_k_head)
    v = jnp.einsum('btl,lhd->bthd', kv_lat, w_uv).astype(jnp.float32)
    n_blk = t // Q_BLOCK
    q_blocks = q.reshape(b, n_blk, Q_BLOCK, N_HEADS, QK_DIM).swapaxes(0, 1)
    q_pos = jnp.arange(t, dtype=jnp.int32).reshape(n_blk, Q_BLOCK)
    k_pos = jnp.arange(t, dtype=jnp.int32)
    scale = QK_DIM ** -0.5

    def one_block(args):
        qb, qp = args
        s = jnp.einsum('bqhd,bkhd->bhqk', qb, k).astype(jnp.float32) * scale
        s = jnp.where(k_pos[None, :] <= qp[:, None], s, -jnp.inf)
        p = jax.nn.softmax(s, axis=-1)
        return jnp.einsum('bhqk,bkhd->bqhd', p, v)

    o = lax.map(one_block, (q_blocks, q_pos))
    return o.swapaxes(0, 1).reshape(b, t, N_HEADS, V_HEAD).astype(q.dtype)

def _attn_sample(q, kv_new, kr_new, cache_kv, cache_kr, page_table, w_uk, w_uv, g_k_head):
    b, s = q.shape[0], q.shape[1]
    scale = QK_DIM ** -0.5
    qf = q.astype(jnp.float32)

    def absorb(carry, kv_blk, kr_blk, mask):
        m, l, acc = carry
        k = _mla_keys(kv_blk, kr_blk, w_uk, g_k_head).astype(jnp.float32)
        sc = jnp.einsum('bshd,bphd->bhsp', qf, k) * scale
        if mask is not None:
            sc = jnp.where(mask, sc, -jnp.inf)
        m_new = jnp.maximum(m, jnp.max(sc, axis=-1))
        corr = jnp.exp(m - m_new)
        p = jnp.exp(sc - m_new[..., None])
        l = l * corr + jnp.sum(p, axis=-1)
        acc = acc * corr[..., None] + jnp.einsum('bhsp,bpl->bhsl', p, kv_blk.astype(jnp.float32))
        return (m_new, l, acc)

    def page_step(carry, pages):
        return absorb(carry, cache_kv[pages], cache_kr[pages], None), None

    init = (jnp.full((b, N_HEADS, s), -jnp.inf, jnp.float32),
            jnp.zeros((b, N_HEADS, s), jnp.float32),
            jnp.zeros((b, N_HEADS, s, KV_LORA), jnp.float32))
    carry, _ = lax.scan(page_step, init, page_table.T)
    causal = jnp.arange(s)[None, :] <= jnp.arange(s)[:, None]
    m, l, acc = absorb(carry, kv_new, kr_new, causal[None, None])
    o_lat = acc / l[..., None]
    return jnp.einsum('bhsl,lhd->bshd', o_lat, w_uv.astype(jnp.float32)).astype(q.dtype)

def _conv_branch(glu_in, buf_prev, w_dw, b_dw, g_cn, b_cn, w_conv_out):
    za, zb = jnp.split(glu_in, 2, axis=-1)
    z = za * jax.nn.sigmoid(zb)
    buf = jnp.concatenate([buf_prev.astype(z.dtype), z], axis=1)
    y = lax.conv_general_dilated(buf, w_dw[:, None, :].astype(buf.dtype), window_strides=(1,),
                                 padding='VALID', dimension_numbers=('NWC', 'WIO', 'NWC'),
                                 feature_group_count=CONV_CH) + b_dw
    y = jax.nn.silu(_layernorm(y, g_cn, b_cn))
    return y @ w_conv_out, buf[:, -CONV_BUF:, :]

def _decoder_layer(x, c, pos, attn_fn, conv_buf, wts):
    sf1, cf1, gf1, sm, cm, gm, sf2, cf2, gf2 = _adaln(c, wts['w_ada'], wts['b_ada'])
    h = x + 0.5 * gf1 * _swiglu(_modulate(_rmsnorm(x, wts['g_norm_ffn1']), sf1, cf1),
                                wts['w_ffn1_in'], wts['w_ffn1_out'])
    u = _modulate(_rmsnorm(h, wts['g_norm_mix']), sm, cm)
    q_a, kv_a, k_pe, glu_in, gate_logits = _split_in(u @ wts['w_in'])
    q = _mla_query(q_a, pos, wts['g_q_lat'], wts['w_uq'], wts['g_q_head'])
    kv_lat, k_rope = _mla_latent(kv_a, k_pe, pos, wts['g_kv_lat'])
    o = attn_fn(q, kv_lat, k_rope)
    a_out = jnp.einsum('bthd,hdo->bto', o, wts['w_attn_out'])
    b_out, new_buf = _conv_branch(glu_in, conv_buf, wts['w_dw'], wts['b_dw'],
                                  wts['g_conv_norm'], wts['b_conv_norm'], wts['w_conv_out'])
    g_a, g_b = jnp.split(gate_logits, N_BRANCH, axis=-1)
    merged = jax.nn.sigmoid(g_a) * a_out + jax.nn.sigmoid(g_b) * b_out
    h = h + gm * (merged @ wts['w_out'])
    y = h + 0.5 * gf2 * _swiglu(_modulate(_rmsnorm(h, wts['g_norm_ffn2']), sf2, cf2),
                                wts['w_ffn2_in'], wts['w_ffn2_out'])
    return y, kv_lat, k_rope, new_buf

def setup_inputs(seed: int = 0) -> dict:
    key = jax.random.key(seed)
    ks = jax.random.split(key, 40)
    f32 = jnp.float32
    n_pages = PAST_LEN // PAGE_SIZE
    n_used = DEC_BATCH * n_pages
    n_pool = n_used + max(1, n_used // 4)

    def w(k, shape, fan_in, mult=1.0):
        return jax.random.normal(k, shape, f32) * (mult * fan_in ** -0.5)

    def gain(k, n):
        return 1.0 + 0.1 * jax.random.normal(k, (n,), f32)

    def bias(k, n):
        return 0.02 * jax.random.normal(k, (n,), f32)

    perm = jax.random.permutation(ks[7], n_pool)[:n_used]
    page_table = perm.reshape(DEC_BATCH, n_pages).astype(jnp.int32)
    return {
        'x_prompt': jax.random.normal(ks[0], (BATCH, SEQ, D_MODEL), f32),
        'x_sample': jax.random.normal(ks[1], (DEC_BATCH, DEC_SEQ, D_MODEL), f32),
        'c_prompt': jax.random.normal(ks[2], (BATCH, D_MODEL), f32),
        'c_sample': jax.random.normal(ks[3], (DEC_BATCH, D_MODEL), f32),
        'cache_kv_latent': jax.random.normal(ks[4], (n_pool, PAGE_SIZE, KV_LORA), f32),
        'cache_k_rope': jax.random.normal(ks[5], (n_pool, PAGE_SIZE, QK_ROPE), f32),
        'state_conv': 0.5 * jax.random.normal(ks[6], (DEC_BATCH, CONV_BUF, CONV_CH), f32),
        'page_table': page_table,
        'w_ada': w(ks[8], (D_MODEL, N_MOD * D_MODEL), D_MODEL, 0.5),
        'b_ada': bias(ks[9], N_MOD * D_MODEL),
        'g_norm_ffn1': gain(ks[10], D_MODEL),
        'w_ffn1_in': w(ks[11], (D_MODEL, 2 * D_FF), D_MODEL),
        'w_ffn1_out': w(ks[12], (D_FF, D_MODEL), D_FF),
        'g_norm_mix': gain(ks[13], D_MODEL),
        'w_in': w(ks[14], (D_MODEL, IN_COLS), D_MODEL),
        'g_q_lat': gain(ks[15], Q_LORA),
        'w_uq': w(ks[16], (Q_LORA, N_HEADS, QK_DIM), Q_LORA),
        'g_q_head': gain(ks[17], QK_DIM),
        'g_kv_lat': gain(ks[18], KV_LORA),
        'w_uk': w(ks[19], (KV_LORA, N_HEADS, QK_NOPE), KV_LORA),
        'w_uv': w(ks[20], (KV_LORA, N_HEADS, V_HEAD), KV_LORA),
        'g_k_head': gain(ks[21], QK_DIM),
        'w_attn_out': w(ks[22], (N_HEADS, V_HEAD, D_MODEL), N_HEADS * V_HEAD),
        'w_dw': w(ks[23], (CONV_WIDTH, CONV_CH), CONV_WIDTH),
        'b_dw': bias(ks[24], CONV_CH),
        'g_conv_norm': gain(ks[25], CONV_CH),
        'b_conv_norm': bias(ks[26], CONV_CH),
        'w_conv_out': w(ks[27], (CONV_CH, D_MODEL), CONV_CH),
        'w_out': w(ks[28], (D_MODEL, D_MODEL), D_MODEL),
        'g_norm_ffn2': gain(ks[29], D_MODEL),
        'w_ffn2_in': w(ks[30], (D_MODEL, 2 * D_FF), D_MODEL),
        'w_ffn2_out': w(ks[31], (D_FF, D_MODEL), D_FF),
    }

def reference(x_prompt, x_sample, c_prompt, c_sample, cache_kv_latent, cache_k_rope, state_conv,
              page_table, w_ada, b_ada, g_norm_ffn1, w_ffn1_in, w_ffn1_out, g_norm_mix, w_in,
              g_q_lat, w_uq, g_q_head, g_kv_lat, w_uk, w_uv, g_k_head, w_attn_out, w_dw, b_dw,
              g_conv_norm, b_conv_norm, w_conv_out, w_out, g_norm_ffn2, w_ffn2_in, w_ffn2_out):
    wts = dict(w_ada=w_ada, b_ada=b_ada, g_norm_ffn1=g_norm_ffn1, w_ffn1_in=w_ffn1_in,
               w_ffn1_out=w_ffn1_out, g_norm_mix=g_norm_mix, w_in=w_in, g_q_lat=g_q_lat,
               w_uq=w_uq, g_q_head=g_q_head, g_kv_lat=g_kv_lat, w_attn_out=w_attn_out,
               w_dw=w_dw, b_dw=b_dw, g_conv_norm=g_conv_norm, b_conv_norm=b_conv_norm,
               w_conv_out=w_conv_out, w_out=w_out, g_norm_ffn2=g_norm_ffn2,
               w_ffn2_in=w_ffn2_in, w_ffn2_out=w_ffn2_out)
    pos_prompt = jnp.arange(x_prompt.shape[1], dtype=jnp.int32)
    pos_sample = jnp.arange(x_sample.shape[1], dtype=jnp.int32) + PAST_LEN

    def attn_prompt(q, kv_lat, k_rope):
        return _attn_prompt(q, kv_lat, k_rope, w_uk, w_uv, g_k_head)

    def attn_sample(q, kv_lat, k_rope):
        return _attn_sample(q, kv_lat, k_rope, cache_kv_latent, cache_k_rope, page_table,
                            w_uk, w_uv, g_k_head)

    conv_zero = jnp.zeros((x_prompt.shape[0], CONV_BUF, CONV_CH), x_prompt.dtype)
    y_prompt, y_sample = x_prompt, x_sample
    for _ in range(DEPTH):
        y_prompt, kv_latent_prompt, k_rope_prompt, conv_state_prompt = _decoder_layer(
            y_prompt, c_prompt, pos_prompt, attn_prompt, conv_zero, wts)
        y_sample, kv_latent_sample, k_rope_sample, conv_state_sample = _decoder_layer(
            y_sample, c_sample, pos_sample, attn_sample, state_conv, wts)
    return (y_prompt, y_sample, kv_latent_prompt, k_rope_prompt, conv_state_prompt,
            kv_latent_sample, k_rope_sample, conv_state_sample)


_drawn_inputs = setup_inputs


def setup_inputs(seed=0):
    import zlib

    import numpy as np

    out = dict(_drawn_inputs(seed))
    spreads = {}
    factors = {'cache_kv_latent': 8.0,
     'cache_k_rope': 8.0,
     'g_norm_ffn1': 3.634,
     'g_q_lat': 8.0,
     'g_q_head': 8.0,
     'w_uk': 2.768,
     'g_k_head': 8.0,
     'b_dw': 8.0,
     'g_conv_norm': 4.616,
     'b_conv_norm': 38.804,
     'g_norm_ffn2': 3.858}
    for name, (base, spread) in spreads.items():
        noise = np.random.default_rng([zlib.crc32(name.encode()), seed]).standard_normal(out[name].shape)
        drawn = base * np.exp(spread * noise) if base else spread * noise
        out[name] = __import__('jax').numpy.asarray(drawn.astype(out[name].dtype))
    for name, factor in factors.items():
        out[name] = (out[name] * factor).astype(out[name].dtype)
    return out
```

```python
from contextlib import ExitStack

import numpy as np

import concourse.bass as bass
from concourse import mybir

F32 = mybir.dt.float32
F32R = mybir.dt.float32r
I32 = mybir.dt.int32
ALU = mybir.AluOpType
ACT = mybir.ActivationFunctionType
AX_X = mybir.AxisListType.X
ds = bass.ds

P = 128
D = 1024
KT = D // P
SEQ = 256
NB = 8
T = SEQ + NB
NT = 3
TILES = [(0, 128), (128, 128), (256, NB)]
H = 16
NOPE, ROPE, VH = 64, 32, 64
QK = NOPE + ROPE
QL, KL = 384, 256
LAT = QL + KL + ROPE
LT = (QL + KL) // P
FF = 2816
FT = FF // P
CW = 31
PAST = 2048
PAGE = 128
NPG = PAST // PAGE
PAGES = NB * NPG
NMOD = 9
NS = 1 + NB
EPS = 1e-6
SCALE = QK ** -0.5
NEG = -1e30
SLOT = 1024

Q_FFN1_IN, Q_FFN1_OUT, Q_QKV, Q_GLU, Q_UQV, Q_GATE, Q_AO, Q_CO, Q_WO, Q_FFN2_IN, Q_FFN2_OUT, Q_END = (
    0, 11, 17, 19, 23, 25, 29, 31, 33, 35, 46, 52)
G_FFN1_IN, G_FFN1_OUT, G_GLU, G_GATE, G_AO, G_CO, G_WO, G_FFN2_IN, G_FFN2_OUT, G_END = (
    0, 11, 15, 19, 27, 31, 35, 39, 50, 54)
SF1, CF1, GF1, SM, CM, GM, SF2, CF2, GF2 = range(NMOD)
V_ADA, V_G1, V_GM, V_G2, V_BDW, V_GCN, V_BCN, V_GQH, V_GKH, V_N = 0, 72, 80, 88, 96, 104, 112, 120, 121, 122
B_GQL, B_GKL, B_GQH, B_GKH, B_N = 0, 384, 640, 736, 832
C_ID, C_MASK, C_ROPE, C_NEW, C_N = 0, 128, 512, 704, 832
OUT_KTS = [(0, 4), (4, 8), (8, 12), (12, 16), (16, 19), (19, 22)]


def constants():
    c = np.zeros((P, C_N), np.float32)
    c[:, C_ID:C_ID + P] = np.eye(P, dtype=np.float32)
    tri = np.where(np.arange(P)[None, :] <= np.arange(P)[:, None], 0.0, NEG)
    c[:, C_MASK:C_MASK + P] = tri
    c[:, C_MASK + 2 * P:C_MASK + 3 * P] = tri
    half = ROPE // 2
    inv = np.float32(10000.0) ** (-np.arange(half, dtype=np.float32) / np.float32(half))
    for t, pos in enumerate([np.arange(128), np.arange(128, 256), np.full(128, PAST)]):
        ang = pos.astype(np.float32)[:, None] * inv.astype(np.float32)[None, :]
        o = C_ROPE + 64 * t
        c[:, o:o + 64] = np.concatenate([np.cos(ang), np.cos(ang), -np.sin(ang), np.sin(ang)], 1)
    for b in range(NB):
        for k in range(NB):
            c[k, C_NEW + b * H:C_NEW + (b + 1) * H] = 0.0 if k == b else NEG
    return c


class Own:

    def __init__(self, eng, sem):
        self.eng, self.sem, self.n, self.i, self.step = eng, sem, 0, None, 0

    def done(self, ins):
        ins.then_inc(self.sem, 1)
        self.n += 1

    def value(self):
        return self.n if self.i is None else self.i * self.step + self.n

    def wait(self):
        self.eng.wait_ge(self.sem, self.value())

    def loop(self, i, step):
        self.i, self.step, self.at = i, step, self.n

    def end(self, trips):
        assert self.n - self.at == self.step, (self.n - self.at, self.step)
        self.n, self.i = self.at + trips * self.step, None


def decoder_layer(nc, x, out):
    ctx = ExitStack()
    with ctx:
        def sem(name):
            return ctx.enter_context(nc.semaphore(name))

        base = [1152]

        def sb(name, shape, dt=F32, at=None):
            size = 4 * int(np.prod(shape[1:]))
            size = (size + 31) // 32 * 32
            if at is None:
                at = base[0]
                base[0] += size
            assert at + size <= 229344, (name, at, size)
            return nc.alloc_sbuf_tensor_at(name, shape, dt, offset=at)

        raw = sb("raw", [P, 4, SLOT])
        wH = sb("wH", [P, 4, SLOT], F32R)
        wL = sb("wL", [P, 4, SLOT], F32R)
        uH = sb("uH", [P, KT, T], F32R)
        uL = sb("uL", [P, KT, T], F32R)
        h = sb("h", [P, KT, T])
        u = sb("u", [P, KT, T])
        const = sb("const", [P, C_N])
        ones = sb("ones", [P, P])
        epsc = sb("epsc", [P, 1])
        vecT = sb("vecT", [P, V_N])
        gbc = sb("gbc", [P, B_N])
        mod = sb("mod", [P, NMOD * KT, NS])
        amod = sb("amod", [P, 3, KT, NS])
        csil = sb("csil", [P, KT, NS])
        wdw = sb("wdw", [P, KT, CW])
        rk = sb("rk", [P, NB, NPG, H])
        rs = sb("rs", [P, T])
        rinv = sb("rinv", [P, T])
        table = sb("table", [1, PAGES], I32)
        ident = const[:, C_ID:C_ID + P]

        W = base[0]
        wukF = sb("wukF", [P, 2, D], at=W)
        wukH = sb("wukH", [P, 2, D], F32R, at=W + 8192)
        wukL = sb("wukL", [P, 2, D], F32R, at=W + 16384)
        qtok = sb("qtok", [P, NT, H, QK], at=W)
        wukT = sb("wukT", [P, H // 2, KL], at=W + 18432)
        wuvF = sb("wuvF", [P, 2, D], at=W)
        yH = sb("yH", [P, KT, T], F32R, at=W)
        yL = sb("yL", [P, KT, T], F32R, at=W + 8448)
        Z = W + 26624
        zbuf = sb("zbuf", [P, KT, CW - 1 + T], at=Z)
        stbuf = sb("stbuf", [P, KT, NB, CW - 1], at=Z + 9408)
        oH = sb("oH", [P, KT, T], F32R, at=Z)
        oL = sb("oL", [P, KT, T], F32R, at=Z + 8448)
        X = Z + 17088
        o = X
        ada = sb("ada", [P, 2, KT, 384], at=o); o += 24576
        kvr = sb("kvr", [P, 8, KL], at=o); o += 8192
        kTH = sb("kTH", [P, 2, KL], F32R, at=o); o += 2048
        kTL = sb("kTL", [P, 2, KL], F32R, at=o); o += 2048
        sqb = sb("sqb", [P, 2, D], at=o); o += 8192
        krr = sb("krr", [P, 8, ROPE], at=o); o += 1024
        krq = sb("krq", [P, 8, ROPE], at=o); o += 1024
        ssr = sb("ssr", [P, 8], at=o); o += 32
        nsum = sb("nsum", [P, 8, H], at=o); o += 512
        crow = sb("crow", [NS, D], at=o); o += 4096
        vrow = sb("vrow", [P, P], at=o); o += 512
        dwrow = sb("dwrow", [CW, D], at=o); o += 4096
        xrow = sb("xrow", [P, 2, D], at=o); o += 8192
        xsrow = sb("xsrow", [NB, D], at=o); o += 4096
        strow = sb("strow", [120, 2, D], at=o); o += 8192
        grow = sb("grow", [1, B_N], at=1152)
        o = X
        aH = sb("aH", [P, FT, T], F32R, at=o); o += FT * T * 4
        aL = sb("aL", [P, FT, T], F32R, at=o); o += FT * T * 4
        sg = sb("sg", [P, 2, T], at=o); o += 2112
        a32 = sb("a32", [P, 2, T], at=o); o += 2112
        o = X
        lat = sb("lat", [P, NT, LAT], at=o)
        latH = sb("latH", [P, LT, T], F32R, at=o + 8064)
        latL = sb("latL", [P, LT, T], F32R, at=o + 8064 + 5280)
        oT = sb("oT", [P, KT, T], at=o)
        mrg = sb("mrg", [P, KT, T], at=o + 8448)
        o += 18624
        qT = sb("qT", [QK, H, SEQ], at=o)
        kT = sb("kT", [QK, H, SEQ], at=o + 16384)
        ktok = [sb(f"ktok{t}", [P, H, QK], at=a) for t, a in enumerate([o, o + 6144, o + 32768])]
        kv2 = [sb(f"kv2_{s}", [P, NPG, KL], at=o + 16384 * s) for s in range(2)]
        sig = sb("sig", [P, 2 * KT, T], at=o)
        dtmp = sb("dtmp", [P, KT, NB, CW - 1], at=o)
        fin = sb("fin", [P, NT, D], at=o)
        o += 32768
        vtok = sb("vtok", [P, 2, D], at=o)
        sS = sb("sS", [P, 2, 384], at=o + 8192)
        pS = sb("pS", [P, 2, 384], at=o + 11264)
        pTs = sb("pTs", [P, 2, 384], at=o + 14336)
        ctmp = sb("ctmp", [P, 2, T], at=o)
        kr2 = sb("kr2", [P, 2, NPG, ROPE], at=o)
        krT = sb("krT", [P, 2, 4, P], at=o + 4096)
        kvT = sb("kvT", [P, 4, KL], at=o + 8192)
        S = sb("S", [P, 2, NPG + 1, H], at=o + 12288)
        Pr = sb("Pr", [P, 2, NPG + 1, H], at=o + 14464)
        o += 17408
        qabs = sb("qabs", [P, NB, 2, H], at=o); o += 1024
        qbd = sb("qbd", [P, NB, 4, H], at=o); o += 2048
        snew = sb("snew", [NB, NB, H], at=o); o += 512
        kvn = sb("kvn", [NB, KL], at=o); o += 1024
        kvTn = sb("kvTn", [P, 2, NB], at=o); o += 64
        krTn = sb("krTn", [ROPE, NB], at=o); o += 32
        qnT = sb("qnT", [P, H // 2, NB], at=o); o += 256
        qrT = sb("qrT", [P, H, NB], at=o); o += 512
        olat = sb("olat", [P, 2, H, NB], at=o); o += 1024
        krope = sb("krope", [P, NT, ROPE], at=o); o += 384
        ss6 = sb("ss6", [P, 6], at=o); o += 32
        ri6 = sb("ri6", [P, 6], at=o); o += 32
        hss = sb("hss", [P, 6, H], at=o); o += 384
        hrs = sb("hrs", [P, 6, H], at=o); o += 384
        gqk = sb("gqk", [P, 1], at=o); o += 32
        gqkb = sb("gqkb", [NB, QK], at=o); o += 384
        nm = sb("nm", [P, 2, 2], at=o); o += 32
        ls = sb("ls", [P, 2, 2], at=o); o += 32
        rl = sb("rl", [P, 2, 2], at=o); o += 32
        mx = sb("mx", [P, 2, H], at=o); o += 128
        gmx = sb("gmx", [P, 2, H], at=o); o += 128
        lsum = sb("lsum", [P, 2, H], at=o); o += 128
        rden = sb("rden", [P, H], at=o); o += 64
        tmp8 = sb("tmp8", [P, 2, NB], at=o); o += 64
        zst = sb("zst", [CW - 1 + NB, D], at=X + 18624 + 32768 + 12288)
        junk = u[:, :, :].rearrange("p a b -> p (a b)")
        qr4 = junk[0:NB, 0:2048].rearrange("p (h r d) -> p h r d", h=H, r=4)
        ropet = sb("ropet", [P, 2, H, ROPE], at=X + 18624 + 32768 + 8192)

        qnrow = sb("qnrow", [NB, H, NOPE], at=X + 18624 + 32768 + 8192)

        PS = ctx.enter_context(nc.psum_tensor("PS", [P, 8, 512], F32))

        in_vec, in_gain, in_wuk, in_x, in_st, in_wuv = map(
            sem, ["in_vec", "in_gain", "in_wuk", "in_x", "in_st", "in_wuv"])
        memz = sem("memz")
        vec_ps, gain_ps, x_ps, st_ps = map(sem, ["vec_ps", "gain_ps", "x_ps", "st_ps"])
        vec_sb, gain_sb, x_sb, st_sb = map(sem, ["vec_sb", "gain_sb", "x_sb", "st_sb"])
        wukh_done, wukl_done = sem("wukh_done"), sem("wukl_done")
        kvr_in = [sem(f"kvr_in{k}") for k in range(8)]
        krr_in, ssr_done = sem("krr_in"), sem("ssr_done")
        kT_ps, kTH_done, kTL_done, kn_ps, knsq_done, knsum_done = map(
            sem, ["kT_ps", "kTH_done", "kTL_done", "kn_ps", "knsq_done", "knsum_done"])
        norm_sum, norm_root = sem("norm_sum"), sem("norm_root")
        ada_in = [sem("ada_in0"), sem("ada_in1")]
        ada_ps, ada_done = sem("ada_ps"), sem("ada_done")
        w_in = [sem(f"w_in{k}") for k in range(4)]
        w_hi, w_lo, w_used = sem("w_hi"), sem("w_lo"), sem("w_used")
        g_free = sem("g_free")
        sq_done, ssq_ps, root_done, un_done, uh_done, u_ready = map(
            sem, ["sq_done", "ssq_ps", "root_done", "un_done", "uh_done", "u_ready"])
        sg_done, prod_done, ah_done = sem("sg_done"), sem("prod_done"), sem("ah_done")
        lat_sq, lat_root, lat_ready = sem("lat_sq"), sem("lat_root"), sem("lat_ready")
        use_ps = sem("use_ps")
        use_act, use_dve = sem("use_act"), sem("use_dve")
        FILLED = {n: i + 1 for i, n in enumerate([0, 1, 2, 3, 4, 5, 6, 14, 15, 16, 17, 18])}
        BY_ACT = {n: i + 1 for i, n in enumerate([4, 5, 6, 7, 8, 9, 10, 11, 12, 13, 14, 15, 17])}
        BY_DVE = {n: i + 1 for i, n in enumerate([0, 1, 2, 3])}

        def filled(eng, n):
            eng.wait_ge(use_ps, FILLED[n])

        def read(eng, n):
            eng.wait_ge(*((use_act, BY_ACT[n]) if n in BY_ACT else (use_dve, BY_DVE[n])))

        latH_done, latL_done, zst_done, z_free = sem("latH_done"), sem("latL_done"), sem("zst_done"), sem("z_free")
        new_sb = sem("new_sb")
        ss6_set, tok_ready, tok_sq, tok_ss, tok_root, tok_done = map(
            sem, ["ss6_set", "tok_ready", "tok_sq", "tok_ss", "tok_root", "tok_done"])
        rest_sb = sem("rest_sb")
        sc_ps, masked, nmax, exp_done, pn_done, pT_ps, pT_sb, pv_ps, o_sb = map(
            sem, ["sc_ps", "masked", "nmax", "exp_done", "pn_done", "pT_ps", "pT_sb", "pv_ps", "o_sb"])
        kv2_in = [[sem(f"kv2_in{s}{g}") for g in range(4)] for s in range(2)]
        krT_ps, krT_sb, t2_ps, kvT_sb, sc2_ps, s_sb, mx_done, gmx_done, sub_done, p_done, lsum_done = map(
            sem, ["krT_ps", "krT_sb", "t2_ps", "kvT_sb", "sc2_ps", "s_sb", "mx_done", "gmx_done",
                  "sub_done", "p_done", "lsum_done"])
        pg_rel, den_ps, ol_done, os_ps, os_sb = map(sem, ["pg_rel", "den_ps", "ol_done", "os_ps", "os_sb"])
        y_done, mean_ps, yc_done, ysq_done, var_ps, ysd_done, yn_done, ysilu_done, yh_done, yl_done = map(
            sem, ["y_done", "mean_ps", "yc_done", "ysq_done", "var_ps", "ysd_done", "yn_done",
                  "ysilu_done", "yh_done", "yl_done"])
        oh_done, ol2_done = sem("oh_done"), sem("ol2_done")
        mrg_done, mh_done, ml_done = sem("mrg_done"), sem("mh_done"), sem("ml_done")
        fin_ps, fin_sb = sem("fin_ps"), sem("fin_sb")
        own_act, own_dve, own_pool = sem("own_act"), sem("own_dve"), sem("own_pool")
        written = sem("written")
        zst_out = sem("zst_out")
        n_written = [0]

        block = ctx.enter_context(nc.Block())

        def wview(w):
            return w.rearrange("(k p) n -> p k n", p=P)

        @block.sync
        def _(sp):
            def chunk(q, k, src, n_k, width, first=False):
                if not first:
                    sp.wait_ge(w_lo, 4 * q + k - 3)
                sp.dma_start(raw[:, k, 0:n_k * width].rearrange("p (k n) -> p k n", k=n_k), src
                             ).then_inc(w_in[k], 16)

            def put(dst, src):
                sp.dma_start(dst, src).then_inc(written, 16)
                n_written[0] += 16

            sp.wait_ge(memz, 1)
            sp.dma_start(const[:, :], x["const"]).then_inc(in_vec, 16)
            sp.dma_start(crow[0:1, :], x["c_prompt"]).then_inc(in_vec, 16)
            sp.dma_start(crow[1:NS, :], x["c_sample"]).then_inc(in_vec, 16)
            rows = [("b_ada", V_ADA), ("g_norm_ffn1", V_G1), ("g_norm_mix", V_GM), ("g_norm_ffn2", V_G2),
                    ("b_dw", V_BDW), ("g_conv_norm", V_GCN), ("b_conv_norm", V_BCN)]
            for name, r in rows:
                v = x[name].rearrange("(r n) -> r n", n=P)
                sp.dma_start(vrow[r:r + v.shape[0], :], v).then_inc(in_vec, 16)
            for name, r in (("g_q_head", V_GQH), ("g_k_head", V_GKH)):
                sp.dma_start(vrow[r:r + 1, 0:QK], x[name].rearrange("(r n) -> r n", r=1)).then_inc(in_vec, 16)
            sp.dma_start(dwrow[:, :], x["w_dw"]).then_inc(in_vec, 16)
            sp.dma_start(wukF[:, :, :], x["w_uk"].rearrange("(k p) h d -> p k (h d)", p=P)).then_inc(in_wuk, 16)
            sp.dma_start(table[:, :], x["page_table"].rearrange("b n -> (b n)").rearrange("(a n) -> a n", a=1)
                         ).then_inc(in_gain, 16)
            for name, at in (("g_q_lat", B_GQL), ("g_kv_lat", B_GKL), ("g_q_head", B_GQH), ("g_k_head", B_GKH)):
                v = x[name].rearrange("(r n) -> r n", r=1)
                sp.dma_start(grow[0:1, at:at + v.shape[1]], v).then_inc(in_gain, 16)
            sp.dma_start(xrow[:, :, :], x["x_prompt"].rearrange("o (t p) n -> p (o t) n", p=P)).then_inc(in_x, 16)
            sp.dma_start(xsrow[:, :], x["x_sample"].rearrange("b o n -> (b o) n")).then_inc(in_x, 16)
            st = x["state_conv"].rearrange("b t n -> (b t) n")
            for i in range(2):
                sp.dma_start(strow[:, i, :], st[120 * i:120 * i + 120, :]).then_inc(in_st, 16)
            put(out["conv_state_sample"][:, 0:CW - 2, :], x["state_conv"][:, 1:CW - 1, :])
            sp.wait_ge(in_gain, 80)

            def page(p):
                return sp.value_load(table[0:1, ds(p, 1)], min_val=0, max_val=x["cache_kv_latent"].shape[0] - 1)

            ada_v = wview(x["w_ada"])

            def norm_pages(i, first):
                for k in range(8):
                    if not first:
                        sp.wait_ge(kT_ps, 8 * i + k - 7)
                        if k == 0:
                            sp.wait_ge(ssr_done, i)
                    pg = page(8 * i + k)
                    sp.dma_start(kvr[:, k, :], x["cache_kv_latent"][ds(pg, 1), :, :].rearrange("o p n -> p (o n)")
                                 ).then_inc(kvr_in[k], 16)
                    sp.dma_start(krr[:, k, :], x["cache_k_rope"][ds(pg, 1), :, :].rearrange("o p n -> p (o n)")
                                 ).then_inc(krr_in, 16)

            def ada_chunks(i, first):
                for s in range(2):
                    if not first:
                        sp.wait_ge(ada_ps, 2 * i + s - 1)
                    for k0 in (0, 4):
                        sp.dma_start(ada[:, s, k0:k0 + 4, :], ada_v[:, k0:k0 + 4, ds((2 * i + s) * 384, 384)]
                                     ).then_inc(ada_in[s], 16)

            norm_pages(0, True)
            ada_chunks(0, True)
            with sp.Fori(1, 12) as i:
                norm_pages(i, False)
                ada_chunks(i, False)
            with sp.Fori(12, 16) as i:
                norm_pages(i, False)

            def ffn_in(q0, w, first):
                v = wview(w)

                def quad(j, first):
                    for k in range(4):
                        col = (k // 2) * FF + 256 * j
                        chunk(q0 + j, k, v[:, 4 * (k % 2):4 * (k % 2) + 4, ds(col, 256)], 4, 256, first)

                if first:
                    quad(0, True)
                with sp.Fori(1 if first else 0, FT // 2) as j:
                    quad(j, False)

            def ffn_out(q0, w):
                v = wview(w)
                with sp.Fori(0, 2) as i:
                    for n in range(12):
                        k0, k1 = OUT_KTS[n % 6]
                        col = 512 * i + 256 * (n // 6)
                        chunk(q0 + 3 * i + n // 4, n % 4, v[:, k0:k1, ds(col, 256)], k1 - k0, 256)

            def pair_stage(q0, v, col0, pairs):
                with sp.Fori(0, pairs // 2) as i:
                    for n in range(4):
                        col = col0 + 512 * i + 256 * (n // 2)
                        chunk(q0 + i, n, v[:, 4 * (n % 2):4 * (n % 2) + 4, ds(col, 256)], 4, 256)

            ffn_in(Q_FFN1_IN, x["w_ffn1_in"], True)
            ffn_out(Q_FFN1_OUT, x["w_ffn1_out"])
            win = wview(x["w_in"])
            with sp.Fori(0, 2) as i:
                for k in range(4):
                    chunk(Q_QKV + i, k, win[:, ds(4 * i + k, 1), 0:LAT], 1, LAT)
            with sp.Fori(0, 4) as j:
                for k in range(4):
                    col = LAT + (k // 2) * D + 256 * j
                    chunk(Q_GLU + j, k, win[:, 4 * (k % 2):4 * (k % 2) + 4, ds(col, 256)], 4, 256)
            sp.wait_ge(lat_ready, NT)
            for t, (t0, n) in enumerate(TILES):
                kv, kr = lat[0:n, t, QL:QL + KL], krope[0:n, t, :]
                if t < 2:
                    put(out["kv_latent_prompt"][0, t0:t0 + n, :], kv)
                    put(out["k_rope_prompt"][0, t0:t0 + n, :], kr)
                else:
                    put(out["kv_latent_sample"].rearrange("b o n -> (b o) n"), kv)
                    put(out["k_rope_sample"].rearrange("b o n -> (b o) n"), kr)
            uq = x["w_uq"].rearrange("(k p) h d -> p k (h d)", p=P)
            uv = x["w_uv"].rearrange("(k p) h d -> p k (h d)", p=P)
            for n in range(6):
                chunk(Q_UQV + n // 4, n % 4, uq[:, :, 256 * n:256 * n + 256], 3, 256)
            for n in range(2):
                chunk(Q_UQV + 1, 2 + n, uv[:, :, 512 * n:512 * n + 512], 2, 512)
            sp.wait_ge(zst_done, 2)
            sp.dma_start(out["conv_state_prompt"][0, :, :], zst[0:CW - 1, :]).then_inc(zst_out, 16)
            sp.dma_start(out["conv_state_sample"][:, CW - 2, :], zst[CW - 1:CW - 1 + NB, :]).then_inc(zst_out, 16)
            gate_col = LAT + 2 * D

            def gate_quad(i):
                for n in range(4):
                    col = gate_col + 512 * i + 256 * (n // 2)
                    chunk(Q_GATE + i, n, win[:, 4 * (n % 2):4 * (n % 2) + 4, ds(col, 256)], 4, 256)

            gate_quad(0)
            sp.wait_ge(tok_done, 5)
            sp.wait_ge(rest_sb, 4)
            sp.dma_start(wuvF[:, :, :], uv).then_inc(in_wuv, 16)
            sp.wait_ge(pv_ps, H)

            def sample_pages(i, s, first):
                b = 2 * i + s
                for g in range(4):
                    if not first:
                        sp.wait_ge(pg_rel, 4 * b + g + 1)
                    for k in range(4):
                        p = 4 * g + k
                        pg = page(NPG * b + p)
                        sp.dma_start(kv2[s][:, p, :], x["cache_kv_latent"][ds(pg, 1), :, :].rearrange("o p n -> p (o n)")
                                     ).then_inc(kv2_in[s][g], 16)
                        sp.dma_start(kr2[:, s, p, :], x["cache_k_rope"][ds(pg, 1), :, :].rearrange("o p n -> p (o n)")
                                     ).then_inc(kv2_in[s][g], 16)

            sample_pages(0, 0, True)
            sample_pages(0, 1, True)
            with sp.Fori(1, 4) as i:
                sample_pages(i, 0, False)
                sample_pages(i, 1, False)
            with sp.Fori(1, 4) as i:
                gate_quad(i)
            pair_stage(Q_AO, wview(x["w_attn_out"].rearrange("h d n -> (h d) n")), 0, 4)
            pair_stage(Q_CO, wview(x["w_conv_out"]), 0, 4)
            pair_stage(Q_WO, wview(x["w_out"]), 0, 4)
            ffn_in(Q_FFN2_IN, x["w_ffn2_in"], False)
            ffn_out(Q_FFN2_OUT, x["w_ffn2_out"])
            for t, (t0, n) in enumerate(TILES):
                sp.wait_ge(fin_sb, t + 1)
                if t < 2:
                    put(out["y_prompt"][0, t0:t0 + n, :], fin[0:n, t, :])
                else:
                    put(out["y_sample"].rearrange("b o n -> (b o) n"), fin[0:n, t, :])
            sp.wait_ge(written, n_written[0])
            sp.wait_ge(zst_out, 32)

        @block.gpsimd
        def _(pool):
            nc.gpsimd.memset(vrow[:, :], 0.0).then_inc(memz, 1)
            nc.gpsimd.memset(ones[:, :], 1.0).then_inc(memz, 1)
            nc.gpsimd.memset(epsc[:, :], EPS).then_inc(memz, 1)
            nc.gpsimd.memset(zbuf[:, :, 0:CW - 1], 0.0).then_inc(memz, 1)
            pool.wait_ge(tok_done, 5)
            nc.gpsimd.memset(qbd[:, :, :, :], 0.0).then_inc(memz, 1)
            pool.wait_ge(pv_ps, H)
            nc.gpsimd.memset(S[:, :, NPG, :], NEG).then_inc(memz, 1)
            for b in range(NB):
                pool.wait_ge(mx_done, b + 1)
                nc.gpsimd.partition_all_reduce(gmx[:, b % 2, :], mx[:, b % 2, :], P, bass.bass_isa.ReduceOp.max
                                               ).then_inc(gmx_done, 1)

        @block.scalar
        def _(act):
            own = Own(act, own_act)
            f = nc.scalar.activation

            def ahead(q, k, width=SLOT):
                act.wait_ge(w_used, 4 * q + k + 1)
                hi(q + 1, k, width)

            def hi(q, k, width):
                act.wait_ge(w_in[k], 16 * q + 16)
                f(wH[:, k, 0:width], raw[:, k, 0:width], ACT.Copy).then_inc(w_hi, 1)

            act.wait_ge(vec_ps, 1)
            f(csil[:, :, :].rearrange("p a b -> p (a b)"), PS[:, 0, 0:KT * NS], ACT.Silu)
            f(vecT[:, :], PS[:, 0, 72:72 + V_N], ACT.Copy)
            f(wdw[:, :, :].rearrange("p a b -> p (a b)"), PS[:, 0, 200:200 + KT * CW], ACT.Copy).then_inc(vec_sb, 1)
            act.wait_ge(in_wuk, 16)
            f(wukH[:, :, :], wukF[:, :, :], ACT.Copy).then_inc(wukh_done, 1)
            act.wait_ge(st_ps, 1)
            for i in range(2):
                for j in range(2):
                    f(stbuf[:, 4 * j:4 * j + 4, 4 * i:4 * i + 4, :].rearrange("p f b t -> p f (b t)"),
                      PS[:, 4 + 2 * i + j, 0:480].rearrange("p (f c) -> p f c", f=4), ACT.Copy).then_inc(st_sb, 1)

            def page_hi(p, s):
                act.wait_ge(kT_ps, p + 1)
                act.wait_ge(kn_ps, p + 1)
                f(kTH[:, s, :], PS[:, s, 0:KL], ACT.Copy).then_inc(kTH_done, 1)

            def page_sq(p, s):
                act.wait_ge(kn_ps, p + 3)
                act.wait_ge(knsum_done, p + 1)
                f(sqb[:, s, :], PS[:, 2 + 2 * s:4 + 2 * s, :], ACT.Square).then_inc(knsq_done, 1)

            def norm_block(i, last):
                for k in range(8):
                    p = 8 * i + k
                    if not (last and k == 7):
                        page_hi(p + 1, (k + 1) % 2)
                    page_sq(p, k % 2)
                act.wait_ge(norm_sum, i + 1)
                f(nsum[:, :, :], nsum[:, :, :], ACT.Sqrt, bias=epsc[:, :], scale=1.0 / QK).then_inc(norm_root, 1)

            act.wait_ge(memz, 4)
            act.sem_inc(knsq_done, 2)
            page_hi(0, 0)
            with act.Fori(0, 15) as i:
                norm_block(i, False)
            norm_block(15, True)
            for k in range(4):
                hi(0, k, SLOT)

            def prenorm(n):
                for kt in range(KT):
                    f(u[:, kt, :], h[:, kt, :], ACT.Square).then_inc(sq_done, 1)
                act.wait_ge(ssq_ps, n + 1)
                f(rs[:, :], PS[:, 2, 0:T], ACT.Sqrt, bias=epsc[:, :], scale=1.0 / D).then_inc(root_done, 1)
                act.wait_ge(un_done, 9 * n + 1)
                f(uH[:, :, SEQ:T], u[:, :, SEQ:T], ACT.Copy).then_inc(uh_done, 1)
                shift = (SF1, SM, SF2)[n]
                for kt in range(KT):
                    act.wait_ge(un_done, 9 * n + kt + 2)
                    f(uH[:, kt, 0:SEQ], u[:, kt, 0:SEQ], ACT.Identity,
                      bias=mod[:, KT * shift + kt, 0:1]).then_inc(uh_done, 1)

            def gated_group(q, f0, func, halves):
                def go(j, b):
                    for k in range(4):
                        ahead(q + j, k)
                    for m in range(2):
                        act.wait_ge(prod_done, f0 + 2 * j + m + 1)
                        f(sg[:, m, :], PS[:, b + 2 + m, 0:T], func).then_inc(sg_done, 1)
                    if halves:
                        for m in range(2):
                            act.wait_ge(prod_done, f0 + 2 * j + m + 3)
                            f(aH[:, ds(2 * j + m, 1), :].rearrange("p o n -> p (o n)"), a32[:, m, :], ACT.Copy
                              ).then_inc(ah_done, 1)
                return go

            def ffn_in(q0, g0, f0):
                go = gated_group(q0, f0, ACT.Silu, True)
                go(0, 4 * (g0 % 2))
                with act.Fori(0, 5) as i:
                    for n in range(2):
                        go(2 * i + 1 + n, 4 * ((g0 + 1 + n) % 2))

            def ffn_out(q0, last):
                for n in range(24):
                    if not (last and n >= 20):
                        k0, k1 = OUT_KTS[(n + 4) % 6]
                        ahead(q0 + n // 4, n % 4, 256 * (k1 - k0))

            act.wait_ge(x_sb, KT)
            prenorm(0)
            ffn_in(Q_FFN1_IN, G_FFN1_IN, 0)
            ffn_out(Q_FFN1_OUT, False)
            act.wait_ge(g_free, G_GLU + 2)
            prenorm(1)

            for q, k in [(Q_QKV + i // 4, i % 4) for i in range(8)]:
                ahead(q, k, LAT if q == Q_QKV else SLOT)
            act.wait_ge(ss6_set, 1)
            for t in (2, 0, 1):
                n = TILES[t][1]
                own.wait()
                f(junk[0:n, 0:QL], PS[0:n, 2 * t, 0:QL], ACT.Square, scale=QL ** -0.5,
                  accum_out=ss6[0:n, 2 * t:2 * t + 1])
                own.done(f(junk[0:n, 512:512 + KL], PS[0:n, 2 * t + 1, 0:KL], ACT.Square, scale=KL ** -0.5,
                           accum_out=ss6[0:n, 2 * t + 1:2 * t + 2]))
            own.wait()
            f(ss6[:, :], ss6[:, :], ACT.Sqrt, bias=epsc[:, :]).then_inc(lat_root, 1)

            go = gated_group(Q_GLU, 2 * (FT // 2), ACT.Sigmoid, False)
            with act.Fori(0, 2) as i:
                for n in range(2):
                    go(2 * i + n, 4 * ((G_GLU + n) % 2))

            filled(act, 0)
            for j in range(2):
                f(latH[:, 3 + j, :], PS[:, j, 0:T], ACT.Copy).then_inc(latH_done, 1)
            for j in range(2):
                f(zst[:, 512 * j:512 * j + 512], PS[0:CW - 1 + NB, 2 + j, :], ACT.Copy).then_inc(zst_done, 1)
            filled(act, 1)
            for j in range(3):
                f(latH[:, j, :], PS[:, 4 + j, 0:T], ACT.Copy).then_inc(latH_done, 1)
            for t in range(NT):
                n = TILES[t][1]
                b = 2 * t
                filled(act, 2 + t // 2)
                i_ = f(ktok[t][0:n, :, 0:NOPE], PS[0:n, b:b + 2, :].rearrange("p a (h d) -> p (a h) d", d=NOPE),
                       ACT.Copy)
                i_.then_inc(tok_ready, 1)

            def head_sq(i, tok, n):
                act.wait_ge(tok_sq, i + 1)
                f(junk[0:n, 0:H * QK], tok, ACT.Square).then_inc(tok_ss, 1)

            def head_root(i, n):
                act.wait_ge(tok_root, 2 * i + 1)
                f(hss[0:n, i, :], hss[0:n, i, :], ACT.Sqrt, bias=epsc[0:n, :], scale=1.0 / QK).then_inc(tok_root, 1)

            for t in range(NT):
                n = TILES[t][1]
                head_sq(t, ktok[t][0:n, :, :], n)
                head_root(t, n)
            filled(act, 4)
            f(wukT[:, :, :].rearrange("p a b -> p (a b)"), PS[:, 0:4, :].rearrange("p a b -> p (a b)"),
              ACT.Copy).then_inc(use_act, 1)
            for t in range(2):
                filled(act, 5 + t)
                b = 4 * ((5 + t) % 2)
                f(kT[:, :, 128 * t:128 * t + 128], PS[0:QK, b:b + 4, :].rearrange("p a (h n) -> p (a h) n", n=128),
                  ACT.Copy).then_inc(use_act, 1)
            for n in range(6):
                ahead(Q_UQV + n // 4, n % 4)
                b = 4 * ((7 + n) % 2)
                for t in range(NT):
                    m = TILES[t][1]
                    i_ = f(qtok[0:m, t, :, :].rearrange("p h d -> p (h d)")[:, 256 * n:256 * n + 256],
                           PS[0:m, b + t, 0:256], ACT.Copy)
                i_.then_inc(use_act, 1)
            for n in range(2):
                ahead(Q_UQV + 1, 2 + n)
            for t in range(2):
                i_ = f(vtok[:, t, :].rearrange("p (c n) -> p c n", c=2), PS[:, 4 + t:8:2, :], ACT.Copy)
            i_.then_inc(use_act, 1)
            for t in range(NT):
                n = TILES[t][1]
                head_sq(NT + t, qtok[0:n, t, :, :].rearrange("p h d -> p (h d)"), n)
                head_root(NT + t, n)
            for t in range(2):
                filled(act, 14 + t)
                if t == 0:
                    act.wait_ge(rest_sb, 1)
                b = 4 * ((14 + t) % 2)
                f(qT[:, :, 128 * t:128 * t + 128], PS[0:QK, b:b + 4, :].rearrange("p a (h n) -> p (a h) n", n=128),
                  ACT.Copy, scale=gqk[0:QK, :]).then_inc(use_act, 1)
            filled(act, 17)
            for m in range(2):
                i_ = f(qabs[:, :, :, m:H:2], PS[:, 4 + m, 0:128].rearrange("p (k h b) -> p b k h", k=2, h=H // 2),
                       ACT.Copy)
            i_.then_inc(use_act, 1)

            def turned(hd):
                act.wait_ge(pT_ps, hd + 1)
                if hd >= 2:
                    act.wait_ge(pv_ps, hd - 1)
                f(pTs[:, hd % 2, :], PS[:, 2 + hd % 2, 0:384], ACT.Copy).then_inc(pT_sb, 1)

            act.wait_ge(zst_out, 32)
            for hd in range(H):
                s = hd % 2
                act.wait_ge(nmax, hd + 1)
                if hd >= 2:
                    act.wait_ge(pT_ps, hd - 1)
                    act.wait_ge(pn_done, hd - 1)
                f(pS[:, s, 0:128], sS[:, s, 0:128], ACT.Exp, bias=nm[:, s, 0:1], accum_out=ls[:, s, 0:1])
                f(pS[:, s, 128:384], sS[:, s, 128:384], ACT.Exp, bias=nm[:, s, 1:2], accum_out=ls[:, s, 1:2]
                  ).then_inc(exp_done, 1)
                if hd >= 1:
                    turned(hd - 1)
            turned(H - 1)

            def turn_pages(b, s):
                act.wait_ge(krT_ps, b + 1)
                f(krT[:, s, :, :].rearrange("p a b -> p (a b)"), PS[:, 0, :], ACT.Copy).then_inc(krT_sb, 1)
                for p in range(NPG):
                    act.wait_ge(t2_ps, NPG * b + p + 1)
                    act.wait_ge(sc2_ps, NPG * b + p + 1)
                    f(kvT[:, p % 4, :], PS[:, 1 + p % 2, 0:KL], ACT.Copy).then_inc(kvT_sb, 1)

            def probabilities(b, s):
                act.wait_ge(sub_done, b + 1)
                act.wait_ge(pg_rel, 4 * b + 4)
                f(Pr[:, s, :, :], S[:, s, :, :], ACT.Exp).then_inc(p_done, 1)

            act.sem_inc(krT_sb, 1)
            turn_pages(0, 0)
            probabilities(0, 0)
            with act.Fori(0, 3) as i:
                turn_pages(2 * i + 1, 1)
                probabilities(2 * i + 1, 1)
                turn_pages(2 * i + 2, 0)
                probabilities(2 * i + 2, 0)
            turn_pages(7, 1)
            probabilities(7, 1)
            act.wait_ge(os_ps, 1)
            f(oT[:, :, SEQ:T], PS[:, 0, 0:64].rearrange("p (f b) -> p f b", b=NB), ACT.Copy).then_inc(os_sb, 1)

            for kt in range(KT):
                if kt == 0:
                    act.wait_ge(os_sb, 1)
                    act.wait_ge(o_sb, H // 2)
                    act.wait_ge(z_free, 1)
                f(oH[:, kt, :], oT[:, kt, :], ACT.Copy).then_inc(oh_done, 1)
            for kt in range(KT):
                act.wait_ge(yc_done, kt + 1)
                f(mrg[:, kt, :], u[:, kt, :], ACT.Square).then_inc(ysq_done, 1)

            def gates(j0, n):
                with act.Fori(j0, j0 + n) as j:
                    for m in range(2):
                        for k in range(2):
                            ahead(Q_GATE + j, 2 * m + k)
                        b = 4 * ((G_GATE + m) % 2)
                        f(sig[:, ds(4 * j + 2 * m, 2), :], PS[:, b:b + 2, 0:T], ACT.Sigmoid).then_inc(g_free, 1)

            gates(0, 2)
            act.wait_ge(var_ps, 1)
            f(rs[:, :], PS[:, 3, 0:T], ACT.Sqrt, bias=epsc[:, :], scale=1.0 / D).then_inc(ysd_done, 1)
            gates(2, 2)
            for kt in range(KT):
                act.wait_ge(yn_done, kt + 1)
                f(u[:, kt, :], u[:, kt, :], ACT.Silu, scale=vecT[:, V_GCN + kt:V_GCN + kt + 1],
                  bias=vecT[:, V_BCN + kt:V_BCN + kt + 1]).then_inc(ysilu_done, 1)
            for kt in range(KT):
                act.wait_ge(ysilu_done, kt + 1)
                f(yH[:, kt, :], u[:, kt, :], ACT.Copy).then_inc(yh_done, 1)
            with act.Fori(0, 2) as j:
                for k in range(4):
                    ahead(Q_AO + j, k)
            with act.Fori(0, 2) as j:
                for m in range(2):
                    for k in range(2):
                        ahead(Q_CO + j, 2 * m + k)
                    act.wait_ge(mrg_done, 2 * j + m + 1)
                    f(uH[:, ds(4 * j + 2 * m, 2), :], mrg[:, ds(4 * j + 2 * m, 2), :], ACT.Copy).then_inc(mh_done, 1)
            with act.Fori(0, 2) as j:
                for k in range(4):
                    ahead(Q_WO + j, k)
            act.wait_ge(g_free, G_FFN2_IN + 2)
            prenorm(2)
            ffn_in(Q_FFN2_IN, G_FFN2_IN, FT + KT)
            ffn_out(Q_FFN2_OUT, True)
            for t in range(NT):
                n = TILES[t][1]
                act.wait_ge(fin_ps, t + 1)
                f(fin[0:n, t, :].rearrange("p (a b) -> p a b", a=2), PS[0:n, 2 * t:2 * t + 2, :], ACT.Copy
                  ).then_inc(fin_sb, 1)

        @block.vector
        def _(dve):
            own = Own(dve, own_dve)
            v = nc.vector

            def ahead(q, k, width=SLOT):
                lo(q + 1, k, width)

            def lo(q, k, width):
                dve.wait_ge(w_hi, 4 * q + k + 1)
                v.tensor_tensor(wL[:, k, 0:width], raw[:, k, 0:width], wH[:, k, 0:width].bitcast(F32),
                                ALU.subtract).then_inc(w_lo, 1)

            dve.sem_inc(kTL_done, 2)
            dve.sem_inc(knsum_done, 2)
            dve.sem_inc(ada_done, 2)
            dve.sem_inc(g_free, 2)
            dve.sem_inc(prod_done, 2)
            dve.wait_ge(gain_ps, 1)
            v.tensor_copy(gbc[:, :], PS[:, 1:3, :].rearrange("p a b -> p (a b)")[:, 0:B_N]).then_inc(gain_sb, 1)
            dve.wait_ge(wukh_done, 1)
            v.tensor_tensor(wukL[:, :, :], wukF[:, :, :], wukH[:, :, :].bitcast(F32), ALU.subtract
                            ).then_inc(wukl_done, 1)
            for kt in range(KT):
                dve.wait_ge(x_ps, kt + 1)
                v.tensor_copy(h[:, kt, :], PS[:, 4 + kt % 4, 0:T]).then_inc(x_sb, 1)
            dve.wait_ge(vec_sb, 1)

            def page_lo(p, s):
                dve.wait_ge(kTH_done, p + 1)
                v.tensor_tensor(kTL[:, s, :], PS[:, s, 0:KL], kTH[:, s, :].bitcast(F32), ALU.subtract
                                ).then_inc(kTL_done, 1)

            rkf = rk[:, :, :, :].rearrange("p b j h -> p (b j) h")

            def norm_block(i, last, with_ada):
                dve.wait_ge(krr_in, 128 * i + 128)
                own.done(v.tensor_tensor(krq[:, :, :], krr[:, :, :], krr[:, :, :], ALU.mult))
                own.wait()
                v.tensor_reduce(ssr[:, :], krq[:, :, :], AX_X, ALU.add).then_inc(ssr_done, 1)
                for k in range(8):
                    p = 8 * i + k
                    if not (last and k == 7):
                        page_lo(p + 1, (k + 1) % 2)
                    dve.wait_ge(knsq_done, p + 3)
                    v.tensor_reduce(nsum[:, k, :], sqb[:, k % 2, :].rearrange("p (h d) -> p h d", h=H),
                                    AX_X, ALU.add).then_inc(knsum_done, 1)
                    if with_ada and k in (3, 7):
                        s = k // 4
                        dve.wait_ge(ada_ps, 2 * i + s + 1)
                        tiles = ds(6 * i + 3 * s, 3)
                        v.tensor_tensor(mod[:, tiles, :], PS[:, 6 + s, 0:27].rearrange("p (a b) -> p a b", b=NS),
                                        vecT[:, tiles].unsqueeze(2).to_broadcast([P, 3, NS]), ALU.add
                                        ).then_inc(ada_done, 1)
                dve.wait_ge(knsum_done, 8 * i + 10)
                dve.wait_ge(ssr_done, i + 1)
                v.tensor_tensor(nsum[:, :, :], nsum[:, :, :], ssr[:, :].unsqueeze(2).to_broadcast([P, 8, H]),
                                ALU.add).then_inc(norm_sum, 1)
                dve.wait_ge(norm_root, i + 1)
                own.done(v.reciprocal(rkf[:, ds(8 * i, 8), :], nsum[:, :, :]))

            page_lo(0, 0)
            with dve.Fori(0, 12) as i:
                own.loop(i, 2)
                norm_block(i, False, True)
                own.end(12)
            with dve.Fori(0, 3) as i:
                own.loop(i, 2)
                norm_block(i + 12, False, False)
                own.end(3)
            norm_block(15, True, False)

            dve.wait_ge(ada_done, 26)
            for n, (part, g) in enumerate(((CF1, V_G1), (CM, V_GM), (CF2, V_G2))):
                own.done(v.scalar_tensor_tensor(
                    out=amod[:, n, :, :], in0=mod[:, KT * part:KT * part + KT, :], scalar=1.0,
                    in1=vecT[:, g:g + KT].unsqueeze(2).to_broadcast([P, KT, NS]), op0=ALU.add, op1=ALU.mult))
            for part in (GF1, GF2):
                m = mod[:, KT * part:KT * part + KT, :]
                own.done(v.tensor_scalar(m, m, 0.5, None, ALU.mult))
            own.wait()
            for k in range(4):
                lo(0, k, SLOT)

            def prenorm(n):
                shift = KT * (SF1, SM, SF2)[n]
                dve.wait_ge(root_done, n + 1)
                own.done(v.reciprocal(rinv[:, :], rs[:, :]))
                own.wait()
                us = u[:, :, SEQ:T]
                own.done(v.tensor_tensor(us, h[:, :, SEQ:T], rinv[:, SEQ:T].unsqueeze(1).to_broadcast([P, KT, NB]),
                                         ALU.mult))
                own.wait()
                own.done(v.tensor_tensor(us, us, amod[:, n, :, 1:NS], ALU.mult))
                own.wait()
                v.tensor_tensor(us, us, mod[:, shift:shift + KT, 1:NS], ALU.add).then_inc(un_done, 1)

                def scaled(kt):
                    v.scalar_tensor_tensor(out=u[:, kt, 0:SEQ], in0=h[:, kt, 0:SEQ], scalar=amod[:, n, kt, 0:1],
                                           in1=rinv[:, 0:SEQ], op0=ALU.mult, op1=ALU.mult).then_inc(un_done, 1)

                scaled(0)
                dve.wait_ge(uh_done, 9 * n + 1)
                v.tensor_tensor(uL[:, :, SEQ:T], us, uH[:, :, SEQ:T].bitcast(F32), ALU.subtract).then_inc(u_ready, 1)
                for kt in range(KT):
                    if kt + 1 < KT:
                        scaled(kt + 1)
                    dve.wait_ge(uh_done, 9 * n + kt + 2)
                    v.scalar_tensor_tensor(out=uL[:, kt, 0:SEQ], in0=u[:, kt, 0:SEQ],
                                           scalar=mod[:, shift + kt, 0:1], in1=uH[:, kt, 0:SEQ].bitcast(F32),
                                           op0=ALU.add, op1=ALU.subtract).then_inc(u_ready, 1)

            def ffn_in(q0, g0, f0, h0):
                def go(j, b):
                    for k in range(4):
                        ahead(q0 + j, k)
                    dve.wait_ge(g_free, g0 + j + 2)
                    for m in range(2):
                        dve.wait_ge(sg_done, f0 + 2 * j + m + 1)
                        dve.wait_ge(ah_done, h0 + 2 * j + m + 1)
                        v.tensor_tensor(a32[:, m, :], sg[:, m, :], PS[:, b + m, 0:T], ALU.mult
                                        ).then_inc(prod_done, 1)
                    for m in range(2):
                        dve.wait_ge(ah_done, h0 + 2 * j + m + 3)
                        t = ds(2 * j + m, 1)
                        i_ = v.tensor_tensor(aL[:, t, :].rearrange("p o n -> p (o n)"), a32[:, m, :],
                                             aH[:, t, :].rearrange("p o n -> p (o n)").bitcast(F32), ALU.subtract)
                    i_.then_inc(g_free, 1)

                go(0, 4 * (g0 % 2))
                with dve.Fori(0, 5) as i:
                    for n in range(2):
                        go(2 * i + 1 + n, 4 * ((g0 + 1 + n) % 2))

            def residual(m, b, gate, g):
                for n in range(2):
                    t = ds(m + n, 1)
                    hp = h[:, t, 0:SEQ].rearrange("p o n -> p (o n)")
                    v.scalar_tensor_tensor(out=hp, in0=PS[:, b + n, 0:SEQ],
                                           scalar=mod[:, ds(gate + m + n, 1), 0:1].rearrange("p o n -> p (o n)"),
                                           in1=hp, op0=ALU.mult, op1=ALU.add)
                dve.wait_ge(g_free, g + 2)
                own.done(v.tensor_tensor(tmp8[:, :, :], PS[:, b:b + 2, SEQ:T], mod[:, ds(gate + m, 2), 1:NS], ALU.mult))
                own.wait()
                hs = h[:, ds(m, 2), SEQ:T]
                v.tensor_tensor(hs, hs, tmp8[:, :, :], ALU.add).then_inc(g_free, 1)

            def ffn_out(q0, g0, gate, last):
                for n in range(24):
                    if not (last and n >= 20):
                        k0, k1 = OUT_KTS[(n + 4) % 6]
                        ahead(q0 + n // 4, n % 4, 256 * (k1 - k0))
                    if n % 6 == 5:
                        dve.wait_ge(w_used, 4 * q0 + n + 1)
                        residual(2 * (n // 6), 4 * ((g0 + n // 6) % 2), KT * gate, g0 + n // 6)

            dve.sem_inc(ah_done, 2)
            prenorm(0)
            ffn_in(Q_FFN1_IN, G_FFN1_IN, 0, 0)
            ffn_out(Q_FFN1_OUT, G_FFN1_OUT, GF1, False)
            prenorm(1)

            v.memset(ss6[:, :], 1.0).then_inc(ss6_set, 1)
            for i in range(8):
                q, k = Q_QKV + i // 4, i % 4
                ahead(q, k, LAT if q == Q_QKV else SLOT)
            dve.wait_ge(lat_root, 1)
            own.done(v.reciprocal(ri6[:, :], ss6[:, :]))
            own.wait()

            def rotate(dst, src, t, n, heads):
                half = ROPE // 2
                cos = const[0:n, C_ROPE + 64 * t:C_ROPE + 64 * t + 32]
                sin = const[0:n, C_ROPE + 64 * t + 32:C_ROPE + 64 * t + 64]
                a, b_ = ropet[0:n, 0, 0:heads, :], ropet[0:n, 1, 0:heads, :]

                def bc(z):
                    return z.unsqueeze(1).to_broadcast([n, heads, z.shape[1]])
                own.done(v.tensor_tensor(a, src, bc(cos), ALU.mult))
                own.done(v.tensor_tensor(b_[:, :, 0:half], src[:, :, half:ROPE], bc(sin[:, 0:half]), ALU.mult))
                own.done(v.tensor_tensor(b_[:, :, half:ROPE], src[:, :, 0:half], bc(sin[:, half:ROPE]), ALU.mult))
                own.wait()
                return v.tensor_tensor(dst, a, b_, ALU.add)

            for i, t in enumerate((2, 0, 1)):
                n = TILES[t][1]
                if i >= 1:
                    dve.wait_ge(lat_ready, i)
                v.scalar_tensor_tensor(out=lat[0:n, t, 0:QL], in0=PS[0:n, 2 * t, 0:QL],
                                       scalar=ri6[0:n, 2 * t:2 * t + 1], in1=gbc[0:n, B_GQL:B_GQL + QL],
                                       op0=ALU.mult, op1=ALU.mult)
                v.scalar_tensor_tensor(out=lat[0:n, t, QL:QL + KL], in0=PS[0:n, 2 * t + 1, 0:KL],
                                       scalar=ri6[0:n, 2 * t + 1:2 * t + 2], in1=gbc[0:n, B_GKL:B_GKL + KL],
                                       op0=ALU.mult, op1=ALU.mult)
                rotate(krope[0:n, t:t + 1, :], PS[0:n, 2 * t + 1, KL:KL + ROPE].unsqueeze(1), t, n, 1
                       ).then_inc(lat_ready, 1)
            dve.wait_ge(lat_ready, NT)
            own.done(v.tensor_copy(kvn[:, :], lat[0:NB, 2, QL:QL + KL]))

            with dve.Fori(0, 2) as i:
                for n in range(2):
                    j = 2 * i + n
                    for k in range(4):
                        ahead(Q_GLU + j, k)
                    b = 4 * ((G_GLU + n) % 2)
                    for m in range(2):
                        dve.wait_ge(sg_done, FT + 2 * j + m + 1)
                        i_ = v.tensor_tensor(zbuf[:, ds(2 * j + m, 1), CW - 1:CW - 1 + T].rearrange("p o n -> p (o n)"),
                                             sg[:, m, :], PS[:, b + m, 0:T], ALU.mult)
                        i_.then_inc(prod_done, 1)
                    dve.wait_ge(prod_done, FT + 2 * j + 4)
                    dve.sem_inc(g_free, 1)

            dve.wait_ge(latH_done, 2)
            for j in range(2):
                v.tensor_tensor(latL[:, 3 + j, :], PS[:, j, 0:T], latH[:, 3 + j, :].bitcast(F32), ALU.subtract
                                ).then_inc(latL_done, 1)
            own.done(v.tensor_copy(kvTn[:, :, :], PS[:, 0:2, SEQ:T]))
            dve.wait_ge(zst_done, 2)
            dve.wait_ge(latL_done, 2)
            own.wait()
            dve.sem_inc(use_dve, 1)
            dve.wait_ge(latH_done, 5)
            for j in range(3):
                v.tensor_tensor(latL[:, j, :], PS[:, 4 + j, 0:T], latH[:, j, :].bitcast(F32), ALU.subtract
                                ).then_inc(latL_done, 1)
            own.done(v.tensor_copy(krTn[:, :], PS[0:ROPE, 7, 0:NB]))
            dve.wait_ge(latL_done, 5)
            own.wait()
            dve.sem_inc(use_dve, 1)
            own.done(v.tensor_tensor(gqk[:, :], vecT[:, V_GQH:V_GQH + 1], vecT[:, V_GKH:V_GKH + 1], ALU.mult))
            own.done(v.tensor_tensor(gqkb[:, :], gbc[0:NB, B_GQH:B_GQH + QK], gbc[0:NB, B_GKH:B_GKH + QK], ALU.mult))
            own.wait()
            own.done(v.tensor_scalar(gqkb[:, :], gqkb[:, :], SCALE, None, ALU.mult))
            v.tensor_scalar(gqk[:, :], gqk[:, :], SCALE, None, ALU.mult).then_inc(rest_sb, 1)

            def head_norm(i, tok3, n, scale_tok=True):
                dve.wait_ge(tok_ss, i + 1)
                v.tensor_reduce(hss[0:n, i, :], junk[0:n, 0:H * QK].rearrange("p (h d) -> p h d", h=H),
                                AX_X, ALU.add).then_inc(tok_root, 1)
                dve.wait_ge(tok_root, 2 * i + 2)
                own.done(v.reciprocal(hrs[0:n, i, :], hss[0:n, i, :]))
                own.wait()
                if scale_tok:
                    return v.tensor_tensor(tok3, tok3, hrs[0:n, i, :].unsqueeze(2).to_broadcast([n, H, QK]), ALU.mult)

            for t in range(NT):
                n = TILES[t][1]
                dve.wait_ge(tok_ready, t + 1)
                own.done(v.tensor_copy(ktok[t][0:n, :, NOPE:QK], krope[0:n, t, :].unsqueeze(1).to_broadcast([n, H, ROPE])))
                own.wait()
                if t >= 1:
                    dve.sem_inc(use_dve, 1)
                dve.sem_inc(tok_sq, 1)
                i_ = head_norm(t, ktok[t][0:n, :, :], n, t < 2)
                if t < 2:
                    i_.then_inc(tok_done, 1)
            for n_ in range(6):
                ahead(Q_UQV + n_ // 4, n_ % 4)
            for n_ in range(2):
                ahead(Q_UQV + 1, 2 + n_)
            for n_ in range(7, 13):
                read(dve, n_)
            for t in range(NT):
                n = TILES[t][1]
                part = qtok[0:n, t, :, NOPE:QK]
                own.done(rotate(part, part, t, n, H))
                own.wait()
                dve.sem_inc(tok_sq, 1)
                i_ = head_norm(NT + t, qtok[0:n, t, :, :], n)
                if t < 2:
                    i_.then_inc(tok_done, 1)
                else:
                    own.done(i_)
                    own.wait()
                    own.done(v.tensor_tensor(qtok[0:n, t, :, :], qtok[0:n, t, :, :],
                                             gqkb[:, :].unsqueeze(1).to_broadcast([n, H, QK]), ALU.mult))
                    own.wait()
                    own.done(v.tensor_copy(qnrow[:, :, :], qtok[0:n, t, :, 0:NOPE]))
                    for r in range(4):
                        own.done(v.tensor_copy(qr4[:, :, r, :], qtok[0:n, t, :, NOPE:QK]))
                    own.wait()
                    dve.sem_inc(tok_done, 1)
            filled(dve, 16)
            own.done(v.tensor_copy(qnT[:, :, :], PS[:, 0, 0:64].rearrange("p (a b) -> p a b", b=NB)))
            own.done(v.tensor_copy(qrT[:, :, :], PS[:, 0, 64:192].rearrange("p (a b) -> p a b", b=NB)))
            own.wait()
            dve.sem_inc(rest_sb, 1)
            dve.wait_ge(memz, 5)
            for j in range(4):
                a = slice(32 * j, 32 * j + 32)
                own.done(v.tensor_copy(qbd[a, :, j, :].rearrange("p b h -> p h b"), qrT[a, :, :]))
            own.wait()
            dve.sem_inc(rest_sb, 1)
            filled(dve, 18)
            own.done(v.tensor_tensor(snew[:, :, :], PS[0:NB, 0, 0:128].rearrange("p (b h) -> p b h", b=NB),
                                     hrs[0:NB, 2, :].unsqueeze(1).to_broadcast([NB, NB, H]), ALU.mult))
            own.wait()
            own.done(v.tensor_tensor(snew[:, :, :], snew[:, :, :],
                                     const[0:NB, C_NEW:C_NEW + 128].rearrange("p (b h) -> p b h", b=NB), ALU.add))
            own.wait()
            dve.sem_inc(rest_sb, 1)

            def mask_max(hd):
                s = hd % 2
                dve.wait_ge(sc_ps, hd + 1)
                if hd >= 2:
                    dve.wait_ge(exp_done, hd - 1)
                v.tensor_tensor(sS[:, s, :], PS[:, s, 0:384], const[:, C_MASK:C_MASK + 384], ALU.add
                                ).then_inc(masked, 1)
                dve.wait_ge(masked, hd + 1)
                v.tensor_reduce(nm[:, s, 0:1], sS[:, s, 0:128], AX_X, ALU.max, negate=True)
                v.tensor_reduce(nm[:, s, 1:2], sS[:, s, 128:384], AX_X, ALU.max, negate=True).then_inc(nmax, 1)

            def conv_start(f_):
                y = u[:, ds(f_, 1), 0:SEQ].rearrange("p o n -> p (o n)")
                own.done(v.tensor_scalar(y, zbuf[:, ds(f_, 1), 0:SEQ].rearrange("p o n -> p (o n)"),
                                         wdw[:, ds(f_, 1), 0:1].rearrange("p o n -> p (o n)"),
                                         vecT[:, ds(V_BDW + f_, 1)], ALU.mult, ALU.add))

            mask_max(0)
            for hd in range(H):
                s = hd % 2
                if hd + 1 < H:
                    mask_max(hd + 1)
                dve.wait_ge(exp_done, hd + 1)
                own.done(v.reciprocal(rl[:, s, :], ls[:, s, :]))
                own.wait()
                v.tensor_scalar(pS[:, s, 0:128], pS[:, s, 0:128], rl[:, s, 0:1], None, ALU.mult)
                v.tensor_scalar(pS[:, s, 128:384], pS[:, s, 128:384], rl[:, s, 1:2], None, ALU.mult
                                ).then_inc(pn_done, 1)
                if hd >= 2 and hd % 2 == 0:
                    dve.wait_ge(pv_ps, hd)
                    v.tensor_copy(oT[:, hd // 2 - 1, 0:SEQ], PS[:, 4 + (hd // 2 - 1) % 2, 0:SEQ]).then_inc(o_sb, 1)
            dve.wait_ge(pv_ps, H)
            v.tensor_copy(oT[:, H // 2 - 1, 0:SEQ], PS[:, 4 + (H // 2 - 1) % 2, 0:SEQ]).then_inc(o_sb, 1)

            def scores(b, s):
                dve.wait_ge(sc2_ps, NPG * b + NPG + 4)
                dve.wait_ge(p_done, b + 1)
                v.tensor_tensor(S[:, s, 0:NPG, :], PS[:, 3 + s, 0:NPG * H].rearrange("p (j h) -> p j h", h=H),
                                rk[:, ds(b, 1), :, :].rearrange("p o j h -> p (o j) h"), ALU.mult).then_inc(s_sb, 1)
                own.done(v.tensor_copy(S[0:NB, s, NPG, :], snew[:, ds(b, 1), :].rearrange("p o h -> p (o h)")))
                own.wait()
                dve.wait_ge(s_sb, b + 3)
                v.tensor_reduce(mx[:, s, :], S[:, s, :, :].rearrange("p j h -> p h j"), AX_X, ALU.max
                                ).then_inc(mx_done, 1)

            def subtract(b, s):
                dve.wait_ge(gmx_done, b + 1)
                sv = S[:, s, :, :]
                v.tensor_tensor(sv, sv, gmx[:, s, :].unsqueeze(1).to_broadcast([P, NPG + 1, H]), ALU.subtract
                                ).then_inc(sub_done, 1)

            def sums(b, s):
                dve.wait_ge(p_done, b + 3)
                v.tensor_reduce(lsum[:, s, :], Pr[:, s, :, :].rearrange("p j h -> p h j"), AX_X, ALU.add
                                ).then_inc(lsum_done, 1)

            def latent_out(b):
                dve.wait_ge(den_ps, b + 1)
                own.done(v.reciprocal(rden[:, :], PS[:, 5, 0:H]))
                own.wait()
                dve.wait_ge(pg_rel, 4 * b + 12)
                v.tensor_tensor(olat[:, :, :, ds(b, 1)].rearrange("p k h o -> p k (h o)"), PS[:, 6:8, 0:H],
                                rden[:, :].unsqueeze(1).to_broadcast([P, 2, H]), ALU.mult).then_inc(ol_done, 1)

            def taps(f_):
                conv_start(f_)
                y = u[:, ds(f_, 1), 0:SEQ].rearrange("p o n -> p (o n)")
                for t in range(1, CW):
                    own.wait()
                    own.done(v.scalar_tensor_tensor(
                        out=y, in0=zbuf[:, ds(f_, 1), t:t + SEQ].rearrange("p o n -> p (o n)"),
                        scalar=wdw[:, ds(f_, 1), t:t + 1].rearrange("p o n -> p (o n)"), in1=y,
                        op0=ALU.mult, op1=ALU.add))

            dve.sem_inc(s_sb, 2)
            dve.sem_inc(p_done, 2)
            dve.sem_inc(ol_done, 1)
            dve.sem_inc(kvT_sb, 2)
            dve.wait_ge(memz, 6)
            scores(0, 0)
            subtract(0, 0)
            sums(0, 0)
            with dve.Fori(0, 3) as i:
                own.loop(i, 2 * (CW + 2))
                for n in range(2):
                    b = 2 * i + n
                    taps(b)
                    scores(b + 1, (n + 1) % 2)
                    subtract(b + 1, (n + 1) % 2)
                    sums(b + 1, (n + 1) % 2)
                    latent_out(b)
                own.end(3)
            taps(6)
            scores(7, 1)
            subtract(7, 1)
            sums(7, 1)
            latent_out(6)
            taps(7)
            latent_out(7)

            ys = u[:, :, SEQ:T]
            dve.wait_ge(pg_rel, 4 * NB + 8)
            own.done(v.tensor_tensor(dtmp[:, :, :, :], stbuf[:, :, :, :],
                                     wdw[:, :, 0:CW - 1].unsqueeze(2).to_broadcast([P, KT, NB, CW - 1]), ALU.mult))
            own.wait()
            own.done(v.tensor_reduce(ys, dtmp[:, :, :, :], AX_X, ALU.add))
            zn = dtmp[:, 0, :, 0:KT].rearrange("p b f -> p f b")
            own.wait()
            own.done(v.tensor_tensor(zn, zbuf[:, :, CW - 1 + SEQ:CW - 1 + T],
                                     wdw[:, :, CW - 1:CW].to_broadcast([P, KT, NB]), ALU.mult))
            own.wait()
            own.done(v.tensor_tensor(ys, ys, zn, ALU.add))
            own.wait()
            v.tensor_tensor(ys, ys, vecT[:, V_BDW:V_BDW + KT].unsqueeze(2).to_broadcast([P, KT, NB]), ALU.add
                            ).then_inc(y_done, 1)
            dve.wait_ge(y_done, 1)
            dve.sem_inc(z_free, 1)

            dve.wait_ge(mean_ps, 1)
            for kt in range(KT):
                v.scalar_tensor_tensor(out=u[:, kt, :], in0=PS[:, 2, 0:T], scalar=-1.0 / D, in1=u[:, kt, :],
                                       op0=ALU.mult, op1=ALU.add).then_inc(yc_done, 1)
            for kt in range(KT):
                dve.wait_ge(oh_done, kt + 1)
                v.tensor_tensor(oL[:, kt, :], oT[:, kt, :], oH[:, kt, :].bitcast(F32), ALU.subtract
                                ).then_inc(ol2_done, 1)
            with dve.Fori(0, 2) as j:
                for k in range(4):
                    ahead(Q_GATE + j, k)
            dve.wait_ge(ysd_done, 1)
            own.done(v.reciprocal(rinv[:, :], rs[:, :]))
            own.wait()
            for kt in range(KT):
                v.tensor_tensor(u[:, kt, :], u[:, kt, :], rinv[:, :], ALU.mult).then_inc(yn_done, 1)
            with dve.Fori(2, 4) as j:
                for k in range(4):
                    ahead(Q_GATE + j, k)
            for kt in range(KT):
                dve.wait_ge(yh_done, kt + 1)
                v.tensor_tensor(yL[:, kt, :], u[:, kt, :], yH[:, kt, :].bitcast(F32), ALU.subtract
                                ).then_inc(yl_done, 1)
            dve.wait_ge(g_free, G_AO + 2)
            with dve.Fori(0, 2) as j:
                for m in range(2):
                    for k in range(2):
                        ahead(Q_AO + j, 2 * m + k)
                    dve.wait_ge(w_used, 4 * (Q_AO + j) + 2 * m + 2)
                    b = 4 * ((G_AO + m) % 2)
                    t = ds(4 * j + 2 * m, 2)
                    v.tensor_tensor(mrg[:, t, :], sig[:, t, :], PS[:, b:b + 2, 0:T], ALU.mult).then_inc(g_free, 1)
            with dve.Fori(0, 2) as j:
                own.loop(j, 2)
                for m in range(2):
                    for k in range(2):
                        ahead(Q_CO + j, 2 * m + k)
                    dve.wait_ge(w_used, 4 * (Q_CO + j) + 2 * m + 2)
                    b = 4 * ((G_CO + m) % 2)
                    t = ds(4 * j + 2 * m, 2)
                    own.done(v.tensor_tensor(ctmp[:, :, :], sig[:, ds(KT + 4 * j + 2 * m, 2), :], PS[:, b:b + 2, 0:T],
                                             ALU.mult))
                    own.wait()
                    v.tensor_tensor(mrg[:, t, :], mrg[:, t, :], ctmp[:, :, :], ALU.add).then_inc(mrg_done, 1)
                    dve.wait_ge(mh_done, 2 * j + m + 1)
                    v.tensor_tensor(uL[:, t, :], mrg[:, t, :], uH[:, t, :].bitcast(F32), ALU.subtract
                                    ).then_inc(g_free, 1)
                own.end(2)
            with dve.Fori(0, 2) as j:
                own.loop(j, 2)
                for m in range(2):
                    for k in range(2):
                        ahead(Q_WO + j, 2 * m + k)
                    dve.wait_ge(w_used, 4 * (Q_WO + j) + 2 * m + 2)
                    residual(4 * j + 2 * m, 4 * ((G_WO + m) % 2), KT * GM, G_WO + 2 * j + m)
                own.end(2)
            prenorm(2)
            ffn_in(Q_FFN2_IN, G_FFN2_IN, FT + KT, FT)
            ffn_out(Q_FFN2_OUT, G_FFN2_OUT, GF2, True)

        @block.tensor
        def _(pe):
            mm = nc.tensor.matmul
            tr = nc.tensor.transpose

            def product(dst, a, b, start, stop):
                mm(dst, a[0], b[0], start=start, stop=False)
                mm(dst, a[0], b[1], start=False, stop=False)
                return mm(dst, a[1], b[0], start=False, stop=stop)

            def pair(q, ks, kts, banks, mov, nk):
                for i, (dq, k) in enumerate(ks):
                    pe.wait_ge(w_lo, 4 * (q + dq) + k + 1)
                    k0, k1 = kts[i]
                    for m in range(2):
                        for kt in range(k0, k1):
                            c = slice((kt - k0) * 256 + 128 * m, (kt - k0) * 256 + 128 * m + 128)
                            i_ = product(PS[:, banks + m, 0:T], (wH[:, k, c], wL[:, k, c]),
                                         (mov[0][:, kt, :], mov[1][:, kt, :]), kt == 0, kt == nk - 1)
                    i_.then_inc(w_used, 1)

            pe.wait_ge(memz, 4)
            pe.wait_ge(in_vec, 16 * 13)
            for kt in range(KT):
                tr(PS[:, 0, NS * kt:NS * kt + NS], crow[:, P * kt:P * kt + P], ident[0:NS, 0:NS])
            tr(PS[:, 0, 72:72 + V_N], vrow[0:V_N, :], ident[0:V_N, 0:V_N])
            for kt in range(KT):
                i_ = tr(PS[:, 0, 200 + CW * kt:200 + CW * kt + CW], dwrow[:, P * kt:P * kt + P], ident[0:CW, 0:CW])
            i_.then_inc(vec_ps, 1)
            pe.wait_ge(in_gain, 80)
            mm(PS[:, 1, :], ones[0:1, :], grow[0:1, 0:512], start=True, stop=True)
            mm(PS[:, 2, 0:B_N - 512], ones[0:1, :], grow[0:1, 512:B_N], start=True, stop=True).then_inc(gain_ps, 1)
            pe.wait_ge(in_x, 32)
            for kt in range(KT):
                if kt >= 4:
                    pe.wait_ge(x_sb, kt - 3)
                c = slice(P * kt, P * kt + P)
                for t in range(2):
                    tr(PS[:, 4 + kt % 4, 128 * t:128 * t + 128], xrow[:, t, c], ident)
                tr(PS[:, 4 + kt % 4, SEQ:T], xsrow[:, c], ident[0:NB, 0:NB]).then_inc(x_ps, 1)
            pe.wait_ge(in_st, 32)
            pe.wait_ge(x_sb, KT)
            for i in range(2):
                for kt in range(KT):
                    i_ = tr(PS[:, 4 + 2 * i + kt // 4, 120 * (kt % 4):120 * (kt % 4) + 120],
                            strow[:, i, P * kt:P * kt + P], ident[0:120, 0:120])
            i_.then_inc(st_ps, 1)
            pe.wait_ge(vec_sb, 1)
            pe.wait_ge(gain_sb, 1)
            pe.wait_ge(st_sb, 4)
            pe.wait_ge(wukl_done, 1)

            pe.sem_inc(kn_ps, 2)

            def turn(p, i, k, s):
                pe.wait_ge(kvr_in[k], 16 * i + 16)
                pe.wait_ge(kTL_done, p + 1)
                tr(PS[:, s, 0:128], kvr[:, k, 0:128], ident)
                tr(PS[:, s, 128:256], kvr[:, k, 128:256], ident).then_inc(kT_ps, 1)

            def keys(p, s):
                pe.wait_ge(kTL_done, p + 3)
                pe.wait_ge(knsq_done, p + 1)
                for c in range(2):
                    for kt in range(2):
                        a = slice(128 * kt, 128 * kt + 128)
                        b = slice(512 * c, 512 * c + 512)
                        i_ = product(PS[:, 2 + 2 * s + c, :], (kTH[:, s, a], kTL[:, s, a]),
                                     (wukH[:, kt, b], wukL[:, kt, b]), kt == 0, kt == 1)
                i_.then_inc(kn_ps, 1)

            def modulation(i, s):
                pe.wait_ge(ada_in[s], 32 * i + 32)
                pe.wait_ge(ada_done, 2 * i + s + 1)
                for m in range(3):
                    for kt in range(KT):
                        i_ = mm(PS[:, 6 + s, NS * m:NS * m + NS], ada[:, s, kt, P * m:P * m + P], csil[:, kt, :],
                                start=(kt == 0), stop=(kt == KT - 1))
                i_.then_inc(ada_ps, 1)

            def norm_block(i, last, with_ada):
                for k in range(8):
                    p = 8 * i + k
                    if k < 7:
                        turn(p + 1, i, k + 1, (k + 1) % 2)
                    elif not last:
                        turn(p + 1, i + 1, 0, 0)
                    keys(p, k % 2)
                    if with_ada and k in (3, 7):
                        modulation(i, k // 4)

            turn(0, 0, 0, 0)
            with pe.Fori(0, 12) as i:
                norm_block(i, False, True)
            with pe.Fori(0, 3) as i:
                norm_block(i + 12, False, False)
            norm_block(15, True, False)

            def prenorm(n):
                for kt in range(KT):
                    pe.wait_ge(sq_done, KT * n + kt + 1)
                    i_ = mm(PS[:, 2, 0:T], ones[:, :], u[:, kt, :], start=(kt == 0), stop=(kt == KT - 1))
                i_.then_inc(ssq_ps, 1)

            def ffn_in(q0, g0):
                ks = [(0, k) for k in range(2)], [(0, k) for k in range(2, 4)]
                kts = [(0, 4), (4, 8)]

                def go(j, b):
                    pe.wait_ge(g_free, g0 + j + 1)
                    pair(q0 + j, ks[0], kts, b, (uH, uL), KT)
                    pair(q0 + j, ks[1], kts, b + 2, (uH, uL), KT)

                go(0, 4 * (g0 % 2))
                with pe.Fori(0, 5) as i:
                    for n in range(2):
                        go(2 * i + 1 + n, 4 * ((g0 + 1 + n) % 2))

            def ffn_out(q0, g0):
                pe.wait_ge(g_free, g0 + 2)
                with pe.Fori(0, 2) as i:
                    for n in range(2):
                        pe.wait_ge(g_free, g0 + 2 * i + n + 1)
                        ks = [((6 * n + c) // 4, (6 * n + c) % 4) for c in range(6)]
                        pair(q0 + 3 * i, ks, OUT_KTS, 4 * ((g0 + n) % 2), (aH, aL), FT)

            def pairs(q0, g0, mov, lo_, hi_):
                with pe.Fori(lo_, hi_) as j:
                    for m in range(2):
                        pe.wait_ge(g_free, g0 + 2 * j + m + 1)
                        pair(q0 + j, [(0, 2 * m), (0, 2 * m + 1)], [(0, 4), (4, 8)], 4 * ((g0 + m) % 2), mov, KT)

            pe.wait_ge(knsq_done, PAGES + 2)
            pe.wait_ge(ada_done, 26)
            prenorm(0)
            pe.wait_ge(u_ready, KT + 1)
            ffn_in(Q_FFN1_IN, G_FFN1_IN)
            ffn_out(Q_FFN1_OUT, G_FFN1_OUT)
            prenorm(1)
            pe.wait_ge(u_ready, 2 * (KT + 1))

            for kt in range(KT):
                q, k = Q_QKV + kt // 4, kt % 4
                pe.wait_ge(w_lo, 4 * q + k + 1)
                for t, (t0, n) in enumerate(TILES):
                    a = (uH[:, kt, t0:t0 + n], uL[:, kt, t0:t0 + n])
                    product(PS[0:n, 2 * t, 0:QL], a, (wH[:, k, 0:QL], wL[:, k, 0:QL]), kt == 0, kt == KT - 1)
                    i_ = product(PS[0:n, 2 * t + 1, 0:LAT - QL], a, (wH[:, k, QL:LAT], wL[:, k, QL:LAT]),
                                 kt == 0, kt == KT - 1)
                i_.then_inc(w_used, 1)

            def glu(j, b):
                pe.wait_ge(g_free, G_GLU + j + 1)
                pair(Q_GLU + j, [(0, 0), (0, 1)], [(0, 4), (4, 8)], b, (uH, uL), KT)
                pair(Q_GLU + j, [(0, 2), (0, 3)], [(0, 4), (4, 8)], b + 2, (uH, uL), KT)

            pe.wait_ge(lat_ready, NT)
            with pe.Fori(0, 2) as i:
                for n in range(2):
                    glu(2 * i + n, 4 * ((G_GLU + n) % 2))
            pe.wait_ge(g_free, G_GATE + 2)

            for j in range(2):
                for t, (t0, n) in enumerate(TILES):
                    tr(PS[:, j, t0:t0 + n], lat[0:n, t, QL + 128 * j:QL + 128 * j + 128], ident[0:n, 0:n])
            for kt in range(KT):
                i_ = tr(PS[0:CW - 1 + NB, 2 + kt // 4, 128 * (kt % 4):128 * (kt % 4) + 128],
                        zbuf[:, kt, SEQ:CW - 1 + T], ident)
            i_.then_inc(use_ps, 1)
            for j in range(3):
                for t, (t0, n) in enumerate(TILES):
                    tr(PS[:, 4 + j, t0:t0 + n], lat[0:n, t, 128 * j:128 * j + 128], ident[0:n, 0:n])
            tr(PS[0:ROPE, 7, 0:NB], krope[0:NB, 2, :], ident[0:NB, 0:NB]).then_inc(use_ps, 1)
            for t, (t0, n) in enumerate(TILES):
                if t == 0:
                    pe.wait_ge(latL_done, 2)
                    read(pe, 0)
                if t == 2:
                    read(pe, 1)
                for c in range(2):
                    for kt in range(2):
                        i_ = product(PS[0:n, 2 * t + c, :],
                                     (latH[:, 3 + kt, t0:t0 + n], latL[:, 3 + kt, t0:t0 + n]),
                                     (wukH[:, kt, 512 * c:512 * c + 512], wukL[:, kt, 512 * c:512 * c + 512]),
                                     kt == 0, kt == 1)
                if t >= 1:
                    i_.then_inc(use_ps, 1)
            read(pe, 2)
            for j in range(H // 2):
                for kt in range(2):
                    at = KL * j + 128 * kt
                    i_ = tr(PS[:, at // 512, at % 512:at % 512 + 128], wukF[:, kt, 128 * j:128 * j + 128], ident)
            i_.then_inc(use_ps, 1)

            def by_head(use, tok):
                b = 4 * (use % 2)
                for hd in range(H):
                    i_ = tr(PS[0:QK, b + hd // 4, 128 * (hd % 4):128 * (hd % 4) + 128], tok[:, hd, :], ident)
                i_.then_inc(use_ps, 1)

            for t in range(2):
                read(pe, 3 + t)
                pe.wait_ge(tok_done, t + 1)
                by_head(5 + t, ktok[t])
            pe.wait_ge(latL_done, 5)
            for n_ in range(6):
                q, k = Q_UQV + n_ // 4, n_ % 4
                read(pe, 5 + n_)
                pe.wait_ge(w_lo, 4 * q + k + 1)
                b = 4 * ((7 + n_) % 2)
                for t, (t0, n) in enumerate(TILES):
                    for kt in range(3):
                        i_ = product(PS[0:n, b + t, 0:256], (latH[:, kt, t0:t0 + n], latL[:, kt, t0:t0 + n]),
                                     (wH[:, k, 256 * kt:256 * kt + 256], wL[:, k, 256 * kt:256 * kt + 256]),
                                     kt == 0, kt == 2)
                i_.then_inc(w_used, 1)
            read(pe, 11)
            for n_ in range(2):
                pe.wait_ge(w_lo, 4 * (Q_UQV + 1) + 2 + n_ + 1)
                for t in range(2):
                    for kt in range(2):
                        c = slice(512 * kt, 512 * kt + 512)
                        i_ = product(PS[:, 4 + 2 * n_ + t, :],
                                     (latH[:, 3 + kt, 128 * t:128 * t + 128], latL[:, 3 + kt, 128 * t:128 * t + 128]),
                                     (wH[:, 2 + n_, c], wL[:, 2 + n_, c]), kt == 0, kt == 1)
                i_.then_inc(w_used, 1)
            for t in range(2):
                read(pe, 12 + t)
                pe.wait_ge(tok_done, 3 + t)
                by_head(14 + t, qtok[:, t, :, :])
            read(pe, 14)
            pe.wait_ge(tok_done, 5)
            for j in range(H // 2):
                tr(PS[:, 0, NB * j:NB * j + NB], qnrow[:, 2 * j:2 * j + 2, :].rearrange("p a d -> p (a d)"), ident[0:NB, 0:NB])
            for hd in range(H):
                i_ = tr(PS[:, 0, 64 + NB * hd:64 + NB * hd + NB],
                        qr4[:, hd, :, :].rearrange("p r d -> p (r d)"), ident[0:NB, 0:NB])
            i_.then_inc(use_ps, 1)
            read(pe, 15)
            pe.wait_ge(rest_sb, 2)
            read(pe, 4)
            for kt in range(2):
                for hd in range(H):
                    a = slice(64 * (hd % 2), 64 * (hd % 2) + 64)
                    at = 64 * kt + NB * (hd // 2)
                    i_ = mm(PS[:, 4 + hd % 2, at:at + NB], wukT[a, hd // 2, 128 * kt:128 * kt + 128], qnT[a, hd // 2, :],
                            start=True, stop=True)
            i_.then_inc(use_ps, 1)
            read(pe, 17)
            pe.wait_ge(rest_sb, 3)
            for kt in range(2):
                mm(PS[0:NB, 0, 0:128], kvTn[:, kt, :], qabs[:, :, kt, :], start=(kt == 0), stop=False)
            mm(PS[0:NB, 0, 0:128], krTn[:, :], qrT[0:ROPE, :, :].rearrange("p h b -> p b h"), start=False, stop=True
               ).then_inc(use_ps, 1)
            pe.wait_ge(rest_sb, 4)

            def scores(hd):
                b = hd % 2
                if hd >= 2:
                    pe.wait_ge(masked, hd - 1)
                mm(PS[:, b, 0:128], qT[:, hd, 0:128], kT[:, hd, 0:128], start=True, stop=True)
                mm(PS[:, b, 128:384], qT[:, hd, 128:256], kT[:, hd, :], start=True, stop=True).then_inc(sc_ps, 1)

            def turn_probs(hd):
                b = 2 + hd % 2
                pe.wait_ge(pn_done, hd + 1)
                if hd >= 2:
                    pe.wait_ge(pT_sb, hd - 1)
                for j in range(3):
                    c = slice(128 * j, 128 * j + 128)
                    i_ = tr(PS[:, b, c], pS[:, hd % 2, c], ident)
                i_.then_inc(pT_ps, 1)

            def values(hd):
                b = 4 + (hd // 2) % 2
                a = slice(64 * (hd % 2), 64 * (hd % 2) + 64)
                vc = slice(VH * hd, VH * hd + VH)
                pe.wait_ge(pT_sb, hd + 1)
                if hd % 2 == 0 and hd >= 4:
                    pe.wait_ge(o_sb, hd // 2 - 1)
                mm(PS[a, b, 0:SEQ], vtok[:, 0, vc], pTs[:, hd % 2, 0:SEQ], start=True, stop=False)
                mm(PS[a, b, 128:SEQ], vtok[:, 1, vc], pTs[:, hd % 2, SEQ:384], start=False, stop=True
                   ).then_inc(pv_ps, 1)

            pe.sem_inc(sc2_ps, 4)
            pe.sem_inc(pg_rel, 8)
            scores(0)
            for hd in range(H):
                if hd + 1 < H:
                    scores(hd + 1)
                turn_probs(hd)
                if hd >= 1:
                    values(hd - 1)
            values(H - 1)

            def page_scores(b, s, use):
                for g in range(4):
                    pe.wait_ge(kv2_in[s][g], 128 * use + 128)
                    if g == 0:
                        pe.wait_ge(krT_sb, b + 1)
                    i_ = tr(PS[:, 0, 128 * g:128 * g + 128],
                            kr2[:, s, 4 * g:4 * g + 4, :].rearrange("p a b -> p (a b)"), ident)
                i_.then_inc(krT_ps, 1)

                def turn2(p):
                    pe.wait_ge(kvT_sb, NPG * b + p + 1)
                    tr(PS[:, 1 + p % 2, 0:128], kv2[s][:, p, 0:128], ident)
                    tr(PS[:, 1 + p % 2, 128:256], kv2[s][:, p, 128:256], ident).then_inc(t2_ps, 1)

                turn2(0)
                pe.wait_ge(s_sb, b + 1)
                for p in range(NPG):
                    if p + 1 < NPG:
                        turn2(p + 1)
                    if p % 4 == 0:
                        if p == 0:
                            pe.wait_ge(krT_sb, b + 2)
                        mm(PS[:, 3 + s, H * p:H * p + 4 * H], krT[:, s, p // 4, :],
                           qbd[:, ds(b, 1), :, :].rearrange("p o j h -> p (o j h)"), start=True, stop=False)
                    pe.wait_ge(kvT_sb, NPG * b + p + 3)
                    for kt in range(2):
                        i_ = mm(PS[:, 3 + s, H * p:H * p + H], kvT[:, p % 4, 128 * kt:128 * kt + 128],
                                qabs[:, ds(b, 1), kt, :].rearrange("p o h -> p (o h)"), start=False,
                                stop=(kt == 1 and p % 4 == 3))
                    i_.then_inc(sc2_ps, 1)

            def page_values(b, s):
                pe.wait_ge(lsum_done, b + 1)
                pe.wait_ge(ol_done, b + 1)
                mm(PS[:, 5, 0:H], ones[:, :], lsum[:, s, :], start=True, stop=True).then_inc(den_ps, 1)
                pe.wait_ge(p_done, b + 3)
                for kt in range(2):
                    mm(PS[:, 6 + kt, 0:H], kvn[:, 128 * kt:128 * kt + 128], Pr[0:NB, s, NPG, :],
                       start=True, stop=False)
                for p in range(NPG):
                    for kt in range(2):
                        i_ = mm(PS[:, 6 + kt, 0:H], kv2[s][:, p, 128 * kt:128 * kt + 128], Pr[:, s, p, :],
                                start=False, stop=(p == NPG - 1))
                    if p % 4 == 3:
                        i_.then_inc(pg_rel, 1)

            pe.wait_ge(o_sb, H // 2)
            page_scores(0, 0, 0)
            with pe.Fori(0, 3) as i:
                page_scores(2 * i + 1, 1, i)
                page_values(2 * i, 0)
                page_scores(2 * i + 2, 0, i + 1)
                page_values(2 * i + 1, 1)
            page_scores(7, 1, 3)
            page_values(6, 0)
            page_values(7, 1)
            pe.wait_ge(ol_done, NB + 1)
            pe.wait_ge(in_wuv, 16)
            for hd in range(H):
                a = slice(64 * (hd % 2), 64 * (hd % 2) + 64)
                for kt in range(2):
                    i_ = mm(PS[a, 0, NB * (hd // 2):NB * (hd // 2) + NB], wuvF[:, kt, VH * hd:VH * hd + VH],
                            olat[:, kt, hd, :], start=(kt == 0), stop=(kt == 1))
            i_.then_inc(os_ps, 1)

            pe.wait_ge(os_sb, 1)
            pe.wait_ge(y_done, 1)
            for kt in range(KT):
                i_ = mm(PS[:, 2, 0:T], ones[:, :], u[:, kt, :], start=(kt == 0), stop=(kt == KT - 1))
            i_.then_inc(mean_ps, 1)
            pairs(Q_GATE, G_GATE, (uH, uL), 0, 2)
            for kt in range(KT):
                pe.wait_ge(ysq_done, kt + 1)
                i_ = mm(PS[:, 3, 0:T], ones[:, :], mrg[:, kt, :], start=(kt == 0), stop=(kt == KT - 1))
            i_.then_inc(var_ps, 1)
            pairs(Q_GATE, G_GATE, (uH, uL), 2, 4)
            pe.wait_ge(ol2_done, KT)
            pairs(Q_AO, G_AO, (oH, oL), 0, 2)
            pe.wait_ge(yl_done, KT)
            pairs(Q_CO, G_CO, (yH, yL), 0, 2)
            pe.wait_ge(g_free, G_WO + 2)
            pairs(Q_WO, G_WO, (uH, uL), 0, 2)
            prenorm(2)
            pe.wait_ge(u_ready, 3 * (KT + 1))
            ffn_in(Q_FFN2_IN, G_FFN2_IN)
            ffn_out(Q_FFN2_OUT, G_FFN2_OUT)
            pe.wait_ge(g_free, G_END + 2)
            for t, (t0, n) in enumerate(TILES):
                for kt in range(KT):
                    i_ = tr(PS[0:n, 2 * t + kt // 4, 128 * (kt % 4):128 * (kt % 4) + 128], h[:, kt, t0:t0 + n], ident)
                i_.then_inc(fin_ps, 1)


INPUTS = ["x_prompt", "x_sample", "c_prompt", "c_sample", "cache_kv_latent", "cache_k_rope", "state_conv",
          "page_table", "w_ada", "b_ada", "g_norm_ffn1", "w_ffn1_in", "w_ffn1_out", "g_norm_mix", "w_in",
          "g_q_lat", "w_uq", "g_q_head", "g_kv_lat", "w_uk", "w_uv", "g_k_head", "w_attn_out", "w_dw", "b_dw",
          "g_conv_norm", "b_conv_norm", "w_conv_out", "w_out", "g_norm_ffn2", "w_ffn2_in", "w_ffn2_out"]
OUTPUTS = [("y_prompt", (1, SEQ, D)), ("y_sample", (NB, 1, D)), ("kv_latent_prompt", (1, SEQ, KL)),
           ("k_rope_prompt", (1, SEQ, ROPE)), ("conv_state_prompt", (1, CW - 1, D)),
           ("kv_latent_sample", (NB, 1, KL)), ("k_rope_sample", (NB, 1, ROPE)),
           ("conv_state_sample", (NB, CW - 1, D))]


def kernel(**inputs):
    import concourse.bacc as bacc
    from concourse.bass_utils import run_bass_kernel_spmd

    nc = bacc.Bacc("TRN2", target_bir_lowering=False, num_devices=1, dynamic_dma_scratch_size=1024)
    arrays = {name: np.ascontiguousarray(inputs[name]) for name in INPUTS}
    arrays["const"] = constants()
    x = {name: nc.dram_tensor(f"in_{name}", a.shape, mybir.dt.from_np(a.dtype), kind="ExternalInput").ap()
         for name, a in arrays.items()}
    out = {name: nc.dram_tensor(f"out_{name}", shape, F32, kind="ExternalOutput").ap() for name, shape in OUTPUTS}
    decoder_layer(nc, x, out)
    r = run_bass_kernel_spmd(nc, [{f"in_{name}": a for name, a in arrays.items()}], core_ids=[0])
    return tuple(r.results[0][f"out_{name}"] for name, _ in OUTPUTS)
```

```python
from contextlib import ExitStack

import numpy as np

import concourse.bass as bass
from concourse import mybir

F32 = mybir.dt.float32
F32R = mybir.dt.float32r
I32 = mybir.dt.int32
ALU = mybir.AluOpType
ACT = mybir.ActivationFunctionType
AX_X = mybir.AxisListType.X
ds = bass.ds

P = 128
D = 1024
KT = D // P
SEQ = 256
NB = 8
T = SEQ + NB
NT = 3
TILES = [(0, 128), (128, 128), (256, NB)]
H = 16
NOPE, ROPE, VH = 64, 32, 64
QK = NOPE + ROPE
QL, KL = 384, 256
LAT = QL + KL + ROPE
LT = (QL + KL) // P
FF = 2816
FT = FF // P
CW = 31
PAST = 2048
PAGE = 128
NPG = PAST // PAGE
PAGES = NB * NPG
NMOD = 9
NS = 1 + NB
EPS = 1e-6
SCALE = QK ** -0.5
NEG = -1e30
SLOT = 1024

Q_ADA, Q_FFN1_IN, Q_FFN1_OUT, Q_QKV, Q_GLU, Q_UQV, Q_GATE, Q_AO, Q_CO, Q_WO, Q_FFN2_IN, Q_FFN2_OUT, Q_END = (
    0, 18, 29, 35, 37, 41, 43, 47, 49, 51, 53, 64, 70)
G_ADA, G_FFN1_IN, G_FFN1_OUT, G_GLU, G_GATE, G_AO, G_CO, G_WO, G_FFN2_IN, G_FFN2_OUT, G_END = (
    0, 36, 47, 51, 55, 63, 67, 71, 75, 86, 90)
SF1, CF1, GF1, SM, CM, GM, SF2, CF2, GF2 = range(NMOD)
V_ADA, V_G1, V_GM, V_G2, V_BDW, V_GCN, V_BCN, V_GQH, V_GKH, V_N = 0, 72, 80, 88, 96, 104, 112, 120, 121, 122
B_GQL, B_GKL, B_GQH, B_GKH, B_N = 0, 384, 640, 736, 832
C_ID, C_MASK, C_ROPE, C_NEW, C_N = 0, 128, 512, 704, 832
OUT_KTS = [(0, 4), (4, 8), (8, 12), (12, 16), (16, 19), (19, 22)]


def constants():
    c = np.zeros((P, C_N), np.float32)
    c[:, C_ID:C_ID + P] = np.eye(P, dtype=np.float32)
    tri = np.where(np.arange(P)[None, :] <= np.arange(P)[:, None], 0.0, NEG)
    c[:, C_MASK:C_MASK + P] = tri
    c[:, C_MASK + 2 * P:C_MASK + 3 * P] = tri
    half = ROPE // 2
    inv = np.float32(10000.0) ** (-np.arange(half, dtype=np.float32) / np.float32(half))
    for t, pos in enumerate([np.arange(128), np.arange(128, 256), np.full(128, PAST)]):
        ang = pos.astype(np.float32)[:, None] * inv.astype(np.float32)[None, :]
        o = C_ROPE + 64 * t
        c[:, o:o + 64] = np.concatenate([np.cos(ang), np.cos(ang), -np.sin(ang), np.sin(ang)], 1)
    for b in range(NB):
        for k in range(NB):
            c[k, C_NEW + b * H:C_NEW + (b + 1) * H] = 0.0 if k == b else NEG
    return c


class Own:

    def __init__(self, eng, sem):
        self.eng, self.sem, self.n, self.i, self.step = eng, sem, 0, None, 0

    def done(self, ins):
        ins.then_inc(self.sem, 1)
        self.n += 1

    def value(self):
        return self.n if self.i is None else self.i * self.step + self.n

    def wait(self):
        self.eng.wait_ge(self.sem, self.value())

    def loop(self, i, step):
        self.i, self.step, self.at = i, step, self.n

    def end(self, trips):
        assert self.n - self.at == self.step, (self.n - self.at, self.step)
        self.n, self.i = self.at + trips * self.step, None


def decoder_layer(nc, x, out):
    ctx = ExitStack()
    with ctx:
        def sem(name):
            return ctx.enter_context(nc.semaphore(name))

        base = [1152]

        def sb(name, shape, dt=F32, at=None):
            size = 4 * int(np.prod(shape[1:]))
            size = (size + 31) // 32 * 32
            if at is None:
                at = base[0]
                base[0] += size
            assert at + size <= 229344, (name, at, size)
            return nc.alloc_sbuf_tensor_at(name, shape, dt, offset=at)

        raw = sb("raw", [P, 4, SLOT])
        wH = sb("wH", [P, 4, SLOT], F32R)
        wL = sb("wL", [P, 4, SLOT], F32R)
        uH = sb("uH", [P, KT, T], F32R)
        uL = sb("uL", [P, KT, T], F32R)
        h = sb("h", [P, KT, T])
        u = sb("u", [P, KT, T])
        const = sb("const", [P, C_N])
        ones = sb("ones", [P, P])
        epsc = sb("epsc", [P, 1])
        vecT = sb("vecT", [P, V_N])
        gbc = sb("gbc", [P, B_N])
        mod = sb("mod", [P, NMOD * KT, NS])
        amod = sb("amod", [P, 3, KT, NS])
        wdw = sb("wdw", [P, KT, CW])
        rs = sb("rs", [P, T])
        rinv = sb("rinv", [P, T])
        table = sb("table", [1, PAGES], I32)
        ident = const[:, C_ID:C_ID + P]

        W = base[0]
        wqH = sb("wqH", [P, 2, H + D + H], F32R, at=W)
        wqL = sb("wqL", [P, 2, H + D + H], F32R, at=W + 8448)
        wukH, wukL = wqH[:, :, H:H + D], wqL[:, :, H:H + D]
        wukF = sb("wukF", [P, 2, D], at=W + 16896)
        wukT = sb("wukT", [P, H // 2, KL], at=W + 16896)
        wuvF = sb("wuvF", [P, 2, D], at=W + 16896)
        yH = sb("yH", [P, KT, T], F32R, at=W)
        yL = sb("yL", [P, KT, T], F32R, at=W + 8448)
        Z = W + 25088
        zbuf = sb("zbuf", [P, KT, CW - 1 + T], at=Z)
        stbuf = sb("stbuf", [P, KT, NB, CW - 1], at=Z + 9408)
        oH = sb("oH", [P, KT, T], F32R, at=Z)
        oL = sb("oL", [P, KT, T], F32R, at=Z + 8448)
        X = Z + 17088
        o = X
        crow = sb("crow", [NS, D], at=o); o += 4096
        vrow = sb("vrow", [P, P], at=o); o += 512
        dwrow = sb("dwrow", [CW, D], at=o); o += 4096
        xrow = sb("xrow", [P, 2, D], at=o); o += 8192
        xsrow = sb("xsrow", [NB, D], at=o); o += 4096
        strow = sb("strow", [120, 2, D], at=o); o += 8192
        grow = sb("grow", [1, B_N], at=o); o += 3328
        csil = sb("csil", [P, KT, NS + 1], at=o); o += 320
        csH = sb("csH", [P, KT, NS + 1], F32R, at=o); o += 320
        csL = sb("csL", [P, KT, NS + 1], F32R, at=o); o += 320
        arow = sb("arow", [P, 2, 256], at=o); o += 2048
        o = X
        aH = sb("aH", [P, FT, T], F32R, at=o); o += FT * T * 4
        aL = sb("aL", [P, FT, T], F32R, at=o); o += FT * T * 4
        sg = sb("sg", [P, 2, T], at=o); o += 2112
        a32 = sb("a32", [P, 2, T], at=o); o += 2112
        o = X
        lat = sb("lat", [P, NT, LAT], at=o)
        latH = sb("latH", [P, LT, T], F32R, at=o + 8064)
        latL = sb("latL", [P, LT, T], F32R, at=o + 8064 + 5280)
        ropet = sb("ropet", [P, 2, H, ROPE], at=o + 8064)
        qnrow = sb("qnrow", [NB, H, NOPE], at=o + 12160)
        oT = sb("oT", [P, KT, T], at=o)
        mrg = sb("mrg", [P, KT, T], at=o + 8448)
        kr2 = sb("kr2", [P, 2, NPG, ROPE], at=o + 8448)
        krT = sb("krT", [P, 2, P], at=o + 12544)
        nsum = sb("nsum", [P, 2, NPG, H], at=o + 13568)
        krq = sb("krq", [P, NPG, ROPE], at=o + 15616)
        ssr = sb("ssr", [P, 2, NPG], at=o + 17664)
        o += 18624
        qT = sb("qT", [QK, H, SEQ], at=o)
        kT = sb("kT", [QK, H, SEQ], at=o + 16384)
        ktok = [sb(f"ktok{t}", [P, H, QK], at=a) for t, a in enumerate([o, o + 6144, o + 16384])]
        qr4 = sb("qr4", [NB, H, 4, ROPE], at=o)
        kv2 = sb("kv2", [P, 2 * NPG, KL], at=o)
        sig = sb("sig", [P, 2 * KT, T], at=o)
        dtmp = sb("dtmp", [P, KT, NB, CW - 1], at=o)
        fin = sb("fin", [P, NT, D], at=o)
        o += 32768
        qtok = sb("qtok", [P, NT, H, QK], at=o)
        sS = sb("sS", [P, 2, 384], at=o + 8192)
        pS = sb("pS", [P, 2, 384], at=o + 11264)
        pTs = sb("pTs", [P, 2, 384], at=o + 14336)
        zst = sb("zst", [CW - 1 + NB, D], at=o)
        ctmp = sb("ctmp", [P, 2, T], at=o)
        sqb = sb("sqb", [P, 2, D], at=o)
        kTH = sb("kTH", [P, 2, KL], F32R, at=o + 8192)
        kTL = sb("kTL", [P, 2, KL], F32R, at=o + 10240)
        S = sb("S", [P, 2, NPG + 1, H], at=o + 12288)
        Pr = sb("Pr", [P, 2, NPG + 1, H], at=o + 14464)
        qabs = sb("qabs", [P, NB, 2, H], at=o + 17408)
        o += 18432
        vtok = sb("vtok", [P, 2, D], at=o)
        olrow = sb("olrow", [H, NB, KL], at=o)
        o += 8192
        qaH = sb("qaH", [P, NB, 2, H], F32R, at=o); o += 1024
        qaL = sb("qaL", [P, NB, 2, H], F32R, at=o); o += 1024
        qbd = sb("qbd", [P, NB, 4, H], at=o); o += 2048
        snew = sb("snew", [NB, NB, H], at=o); o += 512
        kvn = sb("kvn", [NB, KL], at=o); o += 1024
        Srope = sb("Srope", [P, 2, NPG, H], at=o)
        kvTn = sb("kvTn", [P, 2, NB], at=o); o += 64
        krTn = sb("krTn", [ROPE, NB], at=o); o += 32
        qnT = sb("qnT", [P, H // 2, NB], at=o); o += 256
        qrT = sb("qrT", [P, H, NB], at=o); o += 512
        olat = sb("olat", [P, 2, H, NB], at=o); o += 1024 + 160
        krope = sb("krope", [P, NT, ROPE], at=o); o += 384
        ss6 = sb("ss6", [P, 6], at=o); o += 32
        ri6 = sb("ri6", [P, 6], at=o); o += 32
        hss = sb("hss", [P, 6, H], at=o); o += 384
        hrs = sb("hrs", [P, 6, H], at=o); o += 384
        gqk = sb("gqk", [P, 1], at=o); o += 32
        gqkb = sb("gqkb", [NB, QK], at=o); o += 384
        nm = sb("nm", [P, 2, 2], at=o); o += 32
        ls = sb("ls", [P, 2, 2], at=o); o += 32
        rl = sb("rl", [P, 2, 2], at=o); o += 32
        mx = sb("mx", [P, 2, H], at=o); o += 128
        gmx = sb("gmx", [P, 2, H], at=o); o += 128
        lsum = sb("lsum", [P, 2, H], at=o); o += 128
        rden = sb("rden", [H, 1], at=o); o += 32
        tmp8 = sb("tmp8", [P, 2, NB], at=o); o += 64
        junk = u[:, :, :].rearrange("p a b -> p (a b)")

        KEYS = [[(0, 336, 0, 0), (336, 656, 1, H), (656, 1040, 2, H)],
                [(16, 400, 0, 0), (400, 720, 1, 0), (720, 1056, 2, 0)]]
        SQUARES = [[(0, 2, H, 320, 0), (2, 3, H, 384, 640)], [(0, 1, 0, 384, 0), (1, 3, 0, 320, 384)]]
        SCORES = [(0, 0), (2, 320)]

        PS = ctx.enter_context(nc.psum_tensor("PS", [P, 8, 512], F32))

        in_vec, in_gain, in_wuk, in_x, in_st, in_wuv = map(
            sem, ["in_vec", "in_gain", "in_wuk", "in_x", "in_st", "in_wuv"])
        memz = sem("memz")
        vec_ps, gain_ps, x_ps, st_ps = map(sem, ["vec_ps", "gain_ps", "x_ps", "st_ps"])
        vec_sb, gain_sb, x_sb, st_sb = map(sem, ["vec_sb", "gain_sb", "x_sb", "st_sb"])
        wukh_done, wukl_done = sem("wukh_done"), sem("wukl_done")
        arow_done, at_ps = sem("arow_done"), sem("at_ps")
        cs_pad, cs_hi, cs_lo, qah_done = sem("cs_pad"), sem("cs_hi"), sem("cs_lo"), sem("qah_done")
        kT_ps, kTH_done, kTL_done, kn_ps, knsq_done, knsum_done = map(
            sem, ["kT_ps", "kTH_done", "kTL_done", "kn_ps", "knsq_done", "knsum_done"])
        norm_sum, norm_root = sem("norm_sum"), sem("norm_root")
        w_in = [sem(f"w_in{k}") for k in range(4)]
        w_hi, w_lo, w_used = sem("w_hi"), sem("w_lo"), sem("w_used")
        g_free = sem("g_free")
        sq_done, ssq_ps, root_done, un_done, uh_done, u_ready = map(
            sem, ["sq_done", "ssq_ps", "root_done", "un_done", "uh_done", "u_ready"])
        sg_done, prod_done, ah_done = sem("sg_done"), sem("prod_done"), sem("ah_done")
        lat_sq, lat_root, lat_ready = sem("lat_sq"), sem("lat_root"), sem("lat_ready")
        use_ps = sem("use_ps")
        use_act, use_dve = sem("use_act"), sem("use_dve")
        FILLED = {n: i + 1 for i, n in enumerate([0, 1, 2, 3, 4, 5, 6, 14, 15, 16, 17, 18])}
        BY_ACT = {n: i + 1 for i, n in enumerate([4, 5, 6, 7, 8, 9, 10, 11, 12, 13, 15, 17, 18])}
        BY_DVE = {n: i + 1 for i, n in enumerate([0, 1, 2, 3])}

        def filled(eng, n):
            eng.wait_ge(use_ps, FILLED[n])

        def read(eng, n):
            eng.wait_ge(*((use_act, BY_ACT[n]) if n in BY_ACT else (use_dve, BY_DVE[n])))

        latH_done, latL_done, zst_done, z_free = sem("latH_done"), sem("latL_done"), sem("zst_done"), sem("z_free")
        new_sb = sem("new_sb")
        ss6_set, tok_ready, tok_sq, tok_ss, tok_root, tok_done = map(
            sem, ["ss6_set", "tok_ready", "tok_sq", "tok_ss", "tok_root", "tok_done"])
        rest_sb = sem("rest_sb")
        sc_ps, masked, nmax, exp_done, pn_done, pT_ps, pT_sb, pv_ps, o_sb = map(
            sem, ["sc_ps", "masked", "nmax", "exp_done", "pn_done", "pT_ps", "pT_sb", "pv_ps", "o_sb"])
        kv2_in = [sem(f"kv2_in{g}") for g in range(8)]
        qx_done, den_ps, mx_done, gmx_done, sub_done, p_done, lsum_done = map(
            sem, ["qx_done", "den_ps", "mx_done", "gmx_done",
                  "sub_done", "p_done", "lsum_done"])
        pg_rel, ol_done, os_ps, os_sb = map(sem, ["pg_rel", "ol_done", "os_ps", "os_sb"])
        y_done, mean_ps, yc_done, ysq_done, var_ps, ysd_done, yn_done, ysilu_done, yh_done, yl_done = map(
            sem, ["y_done", "mean_ps", "yc_done", "ysq_done", "var_ps", "ysd_done", "yn_done",
                  "ysilu_done", "yh_done", "yl_done"])
        oh_done, ol2_done = sem("oh_done"), sem("ol2_done")
        mrg_done, mh_done, ml_done = sem("mrg_done"), sem("mh_done"), sem("ml_done")
        fin_ps, fin_sb = sem("fin_ps"), sem("fin_sb")
        own_act, own_dve, own_pool = sem("own_act"), sem("own_dve"), sem("own_pool")
        written = sem("written")
        zst_out = sem("zst_out")
        n_written = [0]

        block = ctx.enter_context(nc.Block())

        def wview(w):
            return w.rearrange("(k p) n -> p k n", p=P)

        @block.sync
        def _(sp):
            def chunk(q, k, src, n_k, width, first=False):
                if not first:
                    sp.wait_ge(w_lo, 4 * q + k - 3)
                sp.dma_start(raw[:, k, 0:n_k * width].rearrange("p (k n) -> p k n", k=n_k), src
                             ).then_inc(w_in[k], 16)

            def put(dst, src):
                sp.dma_start(dst, src).then_inc(written, 16)
                n_written[0] += 16

            sp.wait_ge(memz, 1)
            sp.dma_start(const[:, :], x["const"]).then_inc(in_vec, 16)
            sp.dma_start(crow[0:1, :], x["c_prompt"]).then_inc(in_vec, 16)
            sp.dma_start(crow[1:NS, :], x["c_sample"]).then_inc(in_vec, 16)
            rows = [("b_ada", V_ADA), ("g_norm_ffn1", V_G1), ("g_norm_mix", V_GM), ("g_norm_ffn2", V_G2),
                    ("b_dw", V_BDW), ("g_conv_norm", V_GCN), ("b_conv_norm", V_BCN)]
            for name, r in rows:
                v = x[name].rearrange("(r n) -> r n", n=P)
                sp.dma_start(vrow[r:r + v.shape[0], :], v).then_inc(in_vec, 16)
            for name, r in (("g_q_head", V_GQH), ("g_k_head", V_GKH)):
                sp.dma_start(vrow[r:r + 1, 0:QK], x[name].rearrange("(r n) -> r n", r=1)).then_inc(in_vec, 16)
            sp.dma_start(dwrow[:, :], x["w_dw"]).then_inc(in_vec, 16)
            def late_loads():
                sp.dma_start(wukF[:, :, :], x["w_uk"].rearrange("(k p) h d -> p k (h d)", p=P)).then_inc(in_wuk, 16)
                sp.dma_start(table[:, :], x["page_table"].rearrange("b n -> (b n)").rearrange("(a n) -> a n", a=1)
                             ).then_inc(in_gain, 16)
                for name, at in (("g_q_lat", B_GQL), ("g_kv_lat", B_GKL), ("g_q_head", B_GQH), ("g_k_head", B_GKH)):
                    v = x[name].rearrange("(r n) -> r n", r=1)
                    sp.dma_start(grow[0:1, at:at + v.shape[1]], v).then_inc(in_gain, 16)
                sp.dma_start(xrow[:, :, :], x["x_prompt"].rearrange("o (t p) n -> p (o t) n", p=P)).then_inc(in_x, 16)
                sp.dma_start(xsrow[:, :], x["x_sample"].rearrange("b o n -> (b o) n")).then_inc(in_x, 16)
                st = x["state_conv"].rearrange("b t n -> (b t) n")
                for i in range(2):
                    sp.dma_start(strow[:, i, :], st[120 * i:120 * i + 120, :]).then_inc(in_st, 16)
                put(out["conv_state_sample"][:, 0:CW - 2, :], x["state_conv"][:, 1:CW - 1, :])

            def page(p):
                return sp.value_load(table[0:1, ds(p, 1)], min_val=0, max_val=x["cache_kv_latent"].shape[0] - 1)

            ada_v = wview(x["w_ada"])

            def ada_quad(j, first):
                for n in range(4):
                    chunk(Q_ADA + j, n, ada_v[:, 4 * (n % 2):4 * (n % 2) + 4, ds(512 * j + 256 * (n // 2), 256)],
                          4, 256, first)

            ada_quad(0, True)
            late_loads()
            with sp.Fori(1, 18) as j:
                ada_quad(j, False)

            def ffn_in(q0, w):
                v = wview(w)
                with sp.Fori(0, FT // 2) as j:
                    for k in range(4):
                        col = (k // 2) * FF + 256 * j
                        chunk(q0 + j, k, v[:, 4 * (k % 2):4 * (k % 2) + 4, ds(col, 256)], 4, 256)

            def ffn_out(q0, w):
                v = wview(w)
                with sp.Fori(0, 2) as i:
                    for n in range(12):
                        k0, k1 = OUT_KTS[n % 6]
                        col = 512 * i + 256 * (n // 6)
                        chunk(q0 + 3 * i + n // 4, n % 4, v[:, k0:k1, ds(col, 256)], k1 - k0, 256)

            def pair_stage(q0, v, col0, pairs):
                with sp.Fori(0, pairs // 2) as i:
                    for n in range(4):
                        col = col0 + 512 * i + 256 * (n // 2)
                        chunk(q0 + i, n, v[:, 4 * (n % 2):4 * (n % 2) + 4, ds(col, 256)], 4, 256)

            ffn_in(Q_FFN1_IN, x["w_ffn1_in"])
            ffn_out(Q_FFN1_OUT, x["w_ffn1_out"])
            win = wview(x["w_in"])
            with sp.Fori(0, 2) as i:
                for k in range(4):
                    chunk(Q_QKV + i, k, win[:, ds(4 * i + k, 1), 0:LAT], 1, LAT)
            with sp.Fori(0, 4) as j:
                for k in range(4):
                    col = LAT + (k // 2) * D + 256 * j
                    chunk(Q_GLU + j, k, win[:, 4 * (k % 2):4 * (k % 2) + 4, ds(col, 256)], 4, 256)
            sp.wait_ge(lat_ready, NT)
            for t, (t0, n) in enumerate(TILES):
                kv, kr = lat[0:n, t, QL:QL + KL], krope[0:n, t, :]
                if t < 2:
                    put(out["kv_latent_prompt"][0, t0:t0 + n, :], kv)
                    put(out["k_rope_prompt"][0, t0:t0 + n, :], kr)
                else:
                    put(out["kv_latent_sample"].rearrange("b o n -> (b o) n"), kv)
                    put(out["k_rope_sample"].rearrange("b o n -> (b o) n"), kr)
            uq = x["w_uq"].rearrange("(k p) h d -> p k (h d)", p=P)
            uv = x["w_uv"].rearrange("(k p) h d -> p k (h d)", p=P)
            for n in range(6):
                chunk(Q_UQV + n // 4, n % 4, uq[:, :, 256 * n:256 * n + 256], 3, 256)
            for n in range(2):
                chunk(Q_UQV + 1, 2 + n, uv[:, :, 512 * n:512 * n + 512], 2, 512)
            sp.wait_ge(zst_done, 2)
            sp.dma_start(out["conv_state_prompt"][0, :, :], zst[0:CW - 1, :]).then_inc(zst_out, 16)
            sp.dma_start(out["conv_state_sample"][:, CW - 2, :], zst[CW - 1:CW - 1 + NB, :]).then_inc(zst_out, 16)
            gate_col = LAT + 2 * D

            def gate_quad(i):
                for n in range(4):
                    col = gate_col + 512 * i + 256 * (n // 2)
                    chunk(Q_GATE + i, n, win[:, 4 * (n % 2):4 * (n % 2) + 4, ds(col, 256)], 4, 256)

            gate_quad(0)
            sp.wait_ge(rest_sb, 5)
            sp.dma_start(wuvF[:, :, :], uv).then_inc(in_wuv, 16)
            sp.wait_ge(in_gain, 80)
            sp.wait_ge(pv_ps, H)

            def sample_pages(i, s, first):
                b = 2 * i + s
                for g in range(4):
                    if not first:
                        sp.wait_ge(pg_rel, 4 * b + g + 1)
                    for k in range(4):
                        p = 4 * g + k
                        pg = page(NPG * b + p)
                        sp.dma_start(kv2[:, NPG * s + p, :],
                                     x["cache_kv_latent"][ds(pg, 1), :, :].rearrange("o p n -> p (o n)")
                                     ).then_inc(kv2_in[4 * s + g], 16)
                        sp.dma_start(kr2[:, s, p, :],
                                     x["cache_k_rope"][ds(pg, 1), :, :].rearrange("o p n -> p (o n)")
                                     ).then_inc(kv2_in[4 * s + g], 16)

            sample_pages(0, 0, True)
            sample_pages(0, 1, True)
            with sp.Fori(1, 4) as i:
                sample_pages(i, 0, False)
                sample_pages(i, 1, False)
            with sp.Fori(1, 4) as i:
                gate_quad(i)
            pair_stage(Q_AO, wview(x["w_attn_out"].rearrange("h d n -> (h d) n")), 0, 4)
            pair_stage(Q_CO, wview(x["w_conv_out"]), 0, 4)
            pair_stage(Q_WO, wview(x["w_out"]), 0, 4)
            ffn_in(Q_FFN2_IN, x["w_ffn2_in"])
            ffn_out(Q_FFN2_OUT, x["w_ffn2_out"])
            for t, (t0, n) in enumerate(TILES):
                sp.wait_ge(fin_sb, t + 1)
                if t < 2:
                    put(out["y_prompt"][0, t0:t0 + n, :], fin[0:n, t, :])
                else:
                    put(out["y_sample"].rearrange("b o n -> (b o) n"), fin[0:n, t, :])
            sp.wait_ge(written, n_written[0])
            sp.wait_ge(zst_out, 32)

        @block.gpsimd
        def _(pool):
            nc.gpsimd.memset(vrow[:, :], 0.0).then_inc(memz, 1)
            nc.gpsimd.memset(ones[:, :], 1.0).then_inc(memz, 1)
            nc.gpsimd.memset(epsc[:, :], EPS).then_inc(memz, 1)
            nc.gpsimd.memset(arow[:, :, :], 0.0)
            nc.gpsimd.memset(zbuf[:, :, 0:CW - 1], 0.0).then_inc(memz, 1)
            nc.gpsimd.memset(qbd[:, :, :, :], 0.0).then_inc(memz, 1)
            pool.wait_ge(pv_ps, H)
            nc.gpsimd.memset(S[:, :, NPG, :], NEG).then_inc(memz, 1)
            for b in range(NB):
                pool.wait_ge(mx_done, b + 1)
                nc.gpsimd.partition_all_reduce(gmx[:, b % 2, :], mx[:, b % 2, :], P, bass.bass_isa.ReduceOp.max
                                               ).then_inc(gmx_done, 1)

        @block.scalar
        def _(act):
            own = Own(act, own_act)
            f = nc.scalar.activation

            def ahead(q, k, width=SLOT):
                act.wait_ge(w_used, 4 * q + k + 1)
                hi(q + 1, k, width)

            def hi(q, k, width):
                act.wait_ge(w_in[k], 16 * q + 16)
                f(wH[:, k, 0:width], raw[:, k, 0:width], ACT.Copy).then_inc(w_hi, 1)

            act.sem_inc(arow_done, 2)
            act.wait_ge(memz, 4)
            act.wait_ge(vec_ps, 1)
            f(csil[:, :, 0:NS], PS[:, 0, 0:KT * NS].rearrange("p (a b) -> p a b", b=NS), ACT.Silu).then_inc(cs_hi, 1)
            f(vecT[:, :], PS[:, 0, 72:72 + V_N], ACT.Copy)
            f(wdw[:, :, :].rearrange("p a b -> p (a b)"), PS[:, 0, 200:200 + KT * CW], ACT.Copy).then_inc(vec_sb, 1)
            act.wait_ge(cs_hi, 1)
            act.wait_ge(cs_pad, 1)
            f(csH[:, :, :], csil[:, :, :], ACT.Copy).then_inc(cs_hi, 1)
            for k in range(4):
                hi(0, k, SLOT)
            with act.Fori(0, 18) as j:
                for m in range(2):
                    for k in range(2):
                        ahead(Q_ADA + j, 2 * m + k)
                    act.wait_ge(at_ps, 2 * j + m + 1)
                    f(arow[0:NS, m, :], PS[0:NS, 4 * m, 0:256], ACT.Copy).then_inc(arow_done, 1)

            act.wait_ge(in_wuk, 16)
            f(wukH, wukF[:, :, :], ACT.Copy).then_inc(wukh_done, 1)
            act.wait_ge(st_ps, 1)
            for i in range(2):
                for j in range(2):
                    f(stbuf[:, 4 * j:4 * j + 4, 4 * i:4 * i + 4, :].rearrange("p f b t -> p f (b t)"),
                      PS[:, 4 + 2 * i + j, 0:480].rearrange("p (f c) -> p f c", f=4), ACT.Copy).then_inc(st_sb, 1)

            def prenorm(n):
                for kt in range(KT):
                    f(u[:, kt, :], h[:, kt, :], ACT.Square).then_inc(sq_done, 1)
                act.wait_ge(ssq_ps, n + 1)
                f(rs[:, :], PS[:, 2, 0:T], ACT.Sqrt, bias=epsc[:, :], scale=1.0 / D).then_inc(root_done, 1)
                act.wait_ge(un_done, 9 * n + 1)
                f(uH[:, :, SEQ:T], u[:, :, SEQ:T], ACT.Copy).then_inc(uh_done, 1)
                shift = (SF1, SM, SF2)[n]
                for kt in range(KT):
                    act.wait_ge(un_done, 9 * n + kt + 2)
                    f(uH[:, kt, 0:SEQ], u[:, kt, 0:SEQ], ACT.Identity,
                      bias=mod[:, KT * shift + kt, 0:1]).then_inc(uh_done, 1)

            def gated_group(q, f0, func, halves):
                def go(j, b):
                    for k in range(4):
                        ahead(q + j, k)
                    for m in range(2):
                        act.wait_ge(prod_done, f0 + 2 * j + m + 1)
                        f(sg[:, m, :], PS[:, b + 2 + m, 0:T], func).then_inc(sg_done, 1)
                    if halves:
                        for m in range(2):
                            act.wait_ge(prod_done, f0 + 2 * j + m + 3)
                            f(aH[:, ds(2 * j + m, 1), :].rearrange("p o n -> p (o n)"), a32[:, m, :], ACT.Copy
                              ).then_inc(ah_done, 1)
                return go

            def ffn_in(q0, g0, f0):
                go = gated_group(q0, f0, ACT.Silu, True)
                go(0, 4 * (g0 % 2))
                with act.Fori(0, 5) as i:
                    for n in range(2):
                        go(2 * i + 1 + n, 4 * ((g0 + 1 + n) % 2))

            def ffn_out(q0, last):
                for n in range(24):
                    if not (last and n >= 20):
                        k0, k1 = OUT_KTS[(n + 4) % 6]
                        ahead(q0 + n // 4, n % 4, 256 * (k1 - k0))

            act.wait_ge(x_sb, KT)
            prenorm(0)
            ffn_in(Q_FFN1_IN, G_FFN1_IN, 0)
            ffn_out(Q_FFN1_OUT, False)
            act.wait_ge(g_free, G_GLU + 2)
            prenorm(1)

            for q, k in [(Q_QKV + i // 4, i % 4) for i in range(8)]:
                ahead(q, k, LAT if q == Q_QKV else SLOT)
            act.wait_ge(ss6_set, 1)
            for t in (2, 0, 1):
                n = TILES[t][1]
                own.wait()
                f(junk[0:n, 0:QL], PS[0:n, 2 * t, 0:QL], ACT.Square, scale=QL ** -0.5,
                  accum_out=ss6[0:n, 2 * t:2 * t + 1])
                own.done(f(junk[0:n, 512:512 + KL], PS[0:n, 2 * t + 1, 0:KL], ACT.Square, scale=KL ** -0.5,
                           accum_out=ss6[0:n, 2 * t + 1:2 * t + 2]))
            own.wait()
            f(ss6[:, :], ss6[:, :], ACT.Sqrt, bias=epsc[:, :]).then_inc(lat_root, 1)

            go = gated_group(Q_GLU, 2 * (FT // 2), ACT.Sigmoid, False)
            with act.Fori(0, 2) as i:
                for n in range(2):
                    go(2 * i + n, 4 * ((G_GLU + n) % 2))

            filled(act, 0)
            for j in range(2):
                f(latH[:, 3 + j, :], PS[:, j, 0:T], ACT.Copy).then_inc(latH_done, 1)
            for j in range(2):
                f(zst[:, 512 * j:512 * j + 512], PS[0:CW - 1 + NB, 2 + j, :], ACT.Copy).then_inc(zst_done, 1)
            filled(act, 1)
            for j in range(3):
                f(latH[:, j, :], PS[:, 4 + j, 0:T], ACT.Copy).then_inc(latH_done, 1)
            for t in range(NT):
                n = TILES[t][1]
                b = 2 * t
                filled(act, 2 + t // 2)
                i_ = f(ktok[t][0:n, :, 0:NOPE], PS[0:n, b:b + 2, :].rearrange("p a (h d) -> p (a h) d", d=NOPE),
                       ACT.Copy)
                i_.then_inc(tok_ready, 1)

            def head_sq(i, tok, n):
                act.wait_ge(tok_sq, i + 1)
                f(junk[0:n, 0:H * QK], tok, ACT.Square).then_inc(tok_ss, 1)

            def head_root(i, n):
                act.wait_ge(tok_root, 2 * i + 1)
                f(hss[0:n, i, :], hss[0:n, i, :], ACT.Sqrt, bias=epsc[0:n, :], scale=1.0 / QK).then_inc(tok_root, 1)

            for t in range(NT):
                n = TILES[t][1]
                head_sq(t, ktok[t][0:n, :, :], n)
                head_root(t, n)
            filled(act, 4)
            f(wukT[:, :, :].rearrange("p a b -> p (a b)"), PS[:, 0:4, :].rearrange("p a b -> p (a b)"),
              ACT.Copy).then_inc(use_act, 1)
            for t in range(2):
                filled(act, 5 + t)
                b = 4 * ((5 + t) % 2)
                f(kT[:, :, 128 * t:128 * t + 128], PS[0:QK, b:b + 4, :].rearrange("p a (h n) -> p (a h) n", n=128),
                  ACT.Copy).then_inc(use_act, 1)
            act.wait_ge(zst_out, 32)
            for n in range(6):
                ahead(Q_UQV + n // 4, n % 4)
                b = 4 * ((7 + n) % 2)
                for t in range(NT):
                    m = TILES[t][1]
                    i_ = f(qtok[0:m, t, :, :].rearrange("p h d -> p (h d)")[:, 256 * n:256 * n + 256],
                           PS[0:m, b + t, 0:256], ACT.Copy)
                i_.then_inc(use_act, 1)
            for n in range(2):
                ahead(Q_UQV + 1, 2 + n)
            for t in range(2):
                i_ = f(vtok[:, t, :].rearrange("p (c n) -> p c n", c=2), PS[:, 4 + t:8:2, :], ACT.Copy)
            i_.then_inc(use_act, 1)
            for i, t in enumerate((2, 0, 1)):
                n = TILES[t][1]
                if t == 1:
                    filled(act, 15)
                    for m in range(2):
                        i_ = f(qabs[:, :, :, m:H:2],
                               PS[:, 4 + m, 0:128].rearrange("p (k h b) -> p b k h", k=2, h=H // 2), ACT.Copy)
                    i_.then_inc(use_act, 1)
                    act.wait_ge(use_act, BY_ACT[15])
                    f(qaH[:, :, :, :], qabs[:, :, :, :], ACT.Copy).then_inc(qah_done, 1)
                head_sq(NT + i, qtok[0:n, t, :, :].rearrange("p h d -> p (h d)"), n)
                head_root(NT + i, n)
            for t in range(2):
                filled(act, 17 + t)
                if t == 0:
                    act.wait_ge(rest_sb, 1)
                b = 4 * ((17 + t) % 2)
                f(qT[:, :, 128 * t:128 * t + 128], PS[0:QK, b:b + 4, :].rearrange("p a (h n) -> p (a h) n", n=128),
                  ACT.Copy, scale=gqk[0:QK, :]).then_inc(use_act, 1)

            def turned(hd):
                act.wait_ge(pT_ps, hd + 1)
                if hd >= 2:
                    act.wait_ge(pv_ps, hd - 1)
                f(pTs[:, hd % 2, :], PS[:, 2 + hd % 2, 0:384], ACT.Copy).then_inc(pT_sb, 1)

            for hd in range(H):
                s = hd % 2
                act.wait_ge(nmax, hd + 1)
                if hd >= 2:
                    act.wait_ge(pT_ps, hd - 1)
                    act.wait_ge(pn_done, hd - 1)
                f(pS[:, s, 0:128], sS[:, s, 0:128], ACT.Exp, bias=nm[:, s, 0:1], accum_out=ls[:, s, 0:1])
                f(pS[:, s, 128:384], sS[:, s, 128:384], ACT.Exp, bias=nm[:, s, 1:2], accum_out=ls[:, s, 1:2]
                  ).then_inc(exp_done, 1)
                if hd >= 1:
                    turned(hd - 1)
            turned(H - 1)

            def page_hi(pg, n):
                act.wait_ge(kT_ps, pg + 1)
                act.wait_ge(kn_ps, pg + 1)
                if n % 4 == 0:
                    f(krT[:, (n // 4) % 2, :], PS[:, 0, KL:KL + P], ACT.Copy)
                f(kTH[:, n % 2, :], PS[:, 0, 0:KL], ACT.Copy).then_inc(kTH_done, 1)

            def page_sq(pg, n, s, b):
                b0 = 2 + 3 * (n % 2)
                act.wait_ge(kn_ps, pg + 3)
                if n == 0:
                    act.wait_ge(p_done, b + 1)
                bank, c = SCORES[s]
                f(S[:, s, n, :], PS[:, b0 + bank, c:c + H], ACT.Copy)
                act.wait_ge(knsum_done, pg + 1)
                for k0, k1, c, w, at in SQUARES[s]:
                    i_ = f(sqb[:, n % 2, at:at + (k1 - k0) * w].rearrange("p (k w) -> p k w", w=w),
                           PS[:, b0 + k0:b0 + k1, c:c + w], ACT.Square)
                i_.then_inc(knsq_done, 1)

            def norm_roots(b, s):
                act.wait_ge(norm_sum, b + 1)
                f(nsum[:, s, :, :], nsum[:, s, :, :], ACT.Sqrt, bias=epsc[:, :], scale=1.0 / QK).then_inc(norm_root, 1)

            def probabilities(b, s):
                act.wait_ge(sub_done, b + 1)
                act.wait_ge(pg_rel, 4 * b + 4)
                f(Pr[:, s, :, :], S[:, s, :, :], ACT.Exp).then_inc(p_done, 1)

            def sequence(b, s, first=False, last=False):
                for n in range(NPG):
                    pg = NPG * b + n
                    if not (last and n == NPG - 1):
                        page_hi(pg + 1, (n + 1) % NPG)
                    if n == 1 and not first:
                        norm_roots(b - 1, 1 - s)
                    if n == 3 and not first:
                        probabilities(b - 1, 1 - s)
                    page_sq(pg, n, s, b)

            act.sem_inc(knsq_done, 2)
            page_hi(0, 0)
            sequence(0, 0, first=True)
            with act.Fori(0, 3) as i:
                sequence(2 * i + 1, 1)
                sequence(2 * i + 2, 0)
            sequence(7, 1, last=True)
            norm_roots(7, 1)
            probabilities(7, 1)
            act.wait_ge(use_ps, len(FILLED) + 1)
            f(olat[:, :, :, :], PS[:, 0, 0:256].rearrange("p (k b h) -> p k h b", k=2, b=NB), ACT.Copy
              ).then_inc(os_sb, 1)
            act.wait_ge(os_ps, 1)
            f(oT[:, :, SEQ:T], PS[:, 1, 0:64].rearrange("p (f b) -> p f b", b=NB), ACT.Copy).then_inc(os_sb, 1)

            for kt in range(KT):
                if kt == 0:
                    act.wait_ge(os_sb, 2)
                    act.wait_ge(o_sb, H // 2)
                    act.wait_ge(z_free, 1)
                f(oH[:, kt, :], oT[:, kt, :], ACT.Copy).then_inc(oh_done, 1)
            for kt in range(KT):
                act.wait_ge(yc_done, kt + 1)
                f(mrg[:, kt, :], u[:, kt, :], ACT.Square).then_inc(ysq_done, 1)

            def gates(j0, n):
                with act.Fori(j0, j0 + n) as j:
                    for m in range(2):
                        for k in range(2):
                            ahead(Q_GATE + j, 2 * m + k)
                        b = 4 * ((G_GATE + m) % 2)
                        f(sig[:, ds(4 * j + 2 * m, 2), :], PS[:, b:b + 2, 0:T], ACT.Sigmoid).then_inc(g_free, 1)

            gates(0, 2)
            act.wait_ge(var_ps, 1)
            f(rs[:, :], PS[:, 3, 0:T], ACT.Sqrt, bias=epsc[:, :], scale=1.0 / D).then_inc(ysd_done, 1)
            gates(2, 2)
            for kt in range(KT):
                act.wait_ge(yn_done, kt + 1)
                f(u[:, kt, :], u[:, kt, :], ACT.Silu, scale=vecT[:, V_GCN + kt:V_GCN + kt + 1],
                  bias=vecT[:, V_BCN + kt:V_BCN + kt + 1]).then_inc(ysilu_done, 1)
            for kt in range(KT):
                act.wait_ge(ysilu_done, kt + 1)
                f(yH[:, kt, :], u[:, kt, :], ACT.Copy).then_inc(yh_done, 1)
            with act.Fori(0, 2) as j:
                for k in range(4):
                    ahead(Q_AO + j, k)
            with act.Fori(0, 2) as j:
                for m in range(2):
                    for k in range(2):
                        ahead(Q_CO + j, 2 * m + k)
                    act.wait_ge(mrg_done, 2 * j + m + 1)
                    f(uH[:, ds(4 * j + 2 * m, 2), :], mrg[:, ds(4 * j + 2 * m, 2), :], ACT.Copy).then_inc(mh_done, 1)
            with act.Fori(0, 2) as j:
                for k in range(4):
                    ahead(Q_WO + j, k)
            act.wait_ge(g_free, G_FFN2_IN + 2)
            prenorm(2)
            ffn_in(Q_FFN2_IN, G_FFN2_IN, FT + KT)
            ffn_out(Q_FFN2_OUT, True)
            for t in range(NT):
                n = TILES[t][1]
                act.wait_ge(fin_ps, t + 1)
                f(fin[0:n, t, :].rearrange("p (a b) -> p a b", a=2), PS[0:n, 2 * t:2 * t + 2, :], ACT.Copy
                  ).then_inc(fin_sb, 1)

        @block.vector
        def _(dve):
            own = Own(dve, own_dve)
            v = nc.vector

            def ahead(q, k, width=SLOT):
                lo(q + 1, k, width)

            def lo(q, k, width):
                dve.wait_ge(w_hi, 4 * q + k + 1)
                v.tensor_tensor(wL[:, k, 0:width], raw[:, k, 0:width], wH[:, k, 0:width].bitcast(F32),
                                ALU.subtract).then_inc(w_lo, 1)

            dve.sem_inc(kTL_done, 2)
            dve.sem_inc(knsum_done, 2)
            dve.sem_inc(g_free, 2)
            dve.sem_inc(prod_done, 2)
            v.memset(csil[:, :, NS:NS + 1], 0.0).then_inc(cs_pad, 1)
            dve.wait_ge(cs_hi, 2)
            v.tensor_tensor(csL[:, :, :], csil[:, :, :], csH[:, :, :].bitcast(F32), ALU.subtract).then_inc(cs_lo, 1)
            dve.wait_ge(vec_sb, 1)

            for k in range(4):
                lo(0, k, SLOT)
            with dve.Fori(0, 18) as j:
                for m in range(2):
                    for k in range(2):
                        ahead(Q_ADA + j, 2 * m + k)
                    dve.wait_ge(at_ps, 2 * j + m + 3)
                    t = ds(4 * j + 2 * m, 2)
                    v.tensor_tensor(mod[:, t, :], PS[:, 1 + 4 * m, 0:2 * P].rearrange("p (a b) -> p a b", a=2)[:, :, 0:NS], vecT[:, t].unsqueeze(2).to_broadcast([P, 2, NS]),
                                    ALU.add).then_inc(g_free, 1)
            dve.wait_ge(gain_ps, 1)
            v.tensor_copy(gbc[:, :], PS[:, 1:3, :].rearrange("p a b -> p (a b)")[:, 0:B_N]).then_inc(gain_sb, 1)
            dve.wait_ge(wukh_done, 1)
            v.tensor_tensor(wukL, wukF[:, :, :], wukH.bitcast(F32), ALU.subtract
                            ).then_inc(wukl_done, 1)
            for kt in range(KT):
                dve.wait_ge(x_ps, kt + 1)
                v.tensor_copy(h[:, kt, :], PS[:, 4 + kt % 4, 0:T]).then_inc(x_sb, 1)

            dve.wait_ge(g_free, G_FFN1_IN + 2)
            for n, (part, g) in enumerate(((CF1, V_G1), (CM, V_GM), (CF2, V_G2))):
                own.done(v.scalar_tensor_tensor(
                    out=amod[:, n, :, :], in0=mod[:, KT * part:KT * part + KT, :], scalar=1.0,
                    in1=vecT[:, g:g + KT].unsqueeze(2).to_broadcast([P, KT, NS]), op0=ALU.add, op1=ALU.mult))
            for part in (GF1, GF2):
                m = mod[:, KT * part:KT * part + KT, :]
                own.done(v.tensor_scalar(m, m, 0.5, None, ALU.mult))
            own.wait()

            def prenorm(n):
                shift = KT * (SF1, SM, SF2)[n]
                dve.wait_ge(root_done, n + 1)
                own.done(v.reciprocal(rinv[:, :], rs[:, :]))
                own.wait()
                us = u[:, :, SEQ:T]
                own.done(v.tensor_tensor(us, h[:, :, SEQ:T], rinv[:, SEQ:T].unsqueeze(1).to_broadcast([P, KT, NB]),
                                         ALU.mult))
                own.wait()
                own.done(v.tensor_tensor(us, us, amod[:, n, :, 1:NS], ALU.mult))
                own.wait()
                v.tensor_tensor(us, us, mod[:, shift:shift + KT, 1:NS], ALU.add).then_inc(un_done, 1)

                def scaled(kt):
                    v.scalar_tensor_tensor(out=u[:, kt, 0:SEQ], in0=h[:, kt, 0:SEQ], scalar=amod[:, n, kt, 0:1],
                                           in1=rinv[:, 0:SEQ], op0=ALU.mult, op1=ALU.mult).then_inc(un_done, 1)

                scaled(0)
                dve.wait_ge(uh_done, 9 * n + 1)
                v.tensor_tensor(uL[:, :, SEQ:T], us, uH[:, :, SEQ:T].bitcast(F32), ALU.subtract).then_inc(u_ready, 1)
                for kt in range(KT):
                    if kt + 1 < KT:
                        scaled(kt + 1)
                    dve.wait_ge(uh_done, 9 * n + kt + 2)
                    v.scalar_tensor_tensor(out=uL[:, kt, 0:SEQ], in0=u[:, kt, 0:SEQ],
                                           scalar=mod[:, shift + kt, 0:1], in1=uH[:, kt, 0:SEQ].bitcast(F32),
                                           op0=ALU.add, op1=ALU.subtract).then_inc(u_ready, 1)

            def ffn_in(q0, g0, f0, h0):
                def go(j, b):
                    for k in range(4):
                        ahead(q0 + j, k)
                    dve.wait_ge(g_free, g0 + j + 2)
                    for m in range(2):
                        dve.wait_ge(sg_done, f0 + 2 * j + m + 1)
                        dve.wait_ge(ah_done, h0 + 2 * j + m + 1)
                        v.tensor_tensor(a32[:, m, :], sg[:, m, :], PS[:, b + m, 0:T], ALU.mult
                                        ).then_inc(prod_done, 1)
                    for m in range(2):
                        dve.wait_ge(ah_done, h0 + 2 * j + m + 3)
                        t = ds(2 * j + m, 1)
                        i_ = v.tensor_tensor(aL[:, t, :].rearrange("p o n -> p (o n)"), a32[:, m, :],
                                             aH[:, t, :].rearrange("p o n -> p (o n)").bitcast(F32), ALU.subtract)
                    i_.then_inc(g_free, 1)

                go(0, 4 * (g0 % 2))
                with dve.Fori(0, 5) as i:
                    for n in range(2):
                        go(2 * i + 1 + n, 4 * ((g0 + 1 + n) % 2))

            def residual(m, b, gate, g):
                for n in range(2):
                    t = ds(m + n, 1)
                    hp = h[:, t, 0:SEQ].rearrange("p o n -> p (o n)")
                    v.scalar_tensor_tensor(out=hp, in0=PS[:, b + n, 0:SEQ],
                                           scalar=mod[:, ds(gate + m + n, 1), 0:1].rearrange("p o n -> p (o n)"),
                                           in1=hp, op0=ALU.mult, op1=ALU.add)
                dve.wait_ge(g_free, g + 2)
                own.done(v.tensor_tensor(tmp8[:, :, :], PS[:, b:b + 2, SEQ:T], mod[:, ds(gate + m, 2), 1:NS], ALU.mult))
                own.wait()
                hs = h[:, ds(m, 2), SEQ:T]
                v.tensor_tensor(hs, hs, tmp8[:, :, :], ALU.add).then_inc(g_free, 1)

            def ffn_out(q0, g0, gate, last):
                for n in range(24):
                    if not (last and n >= 20):
                        k0, k1 = OUT_KTS[(n + 4) % 6]
                        ahead(q0 + n // 4, n % 4, 256 * (k1 - k0))
                    if n % 6 == 5:
                        dve.wait_ge(w_used, 4 * q0 + n + 1)
                        residual(2 * (n // 6), 4 * ((g0 + n // 6) % 2), KT * gate, g0 + n // 6)

            dve.sem_inc(ah_done, 2)
            prenorm(0)
            ffn_in(Q_FFN1_IN, G_FFN1_IN, 0, 0)
            ffn_out(Q_FFN1_OUT, G_FFN1_OUT, GF1, False)
            prenorm(1)

            v.memset(ss6[:, :], 1.0).then_inc(ss6_set, 1)
            for i in range(8):
                q, k = Q_QKV + i // 4, i % 4
                ahead(q, k, LAT if q == Q_QKV else SLOT)
            dve.wait_ge(lat_root, 1)
            own.done(v.reciprocal(ri6[:, :], ss6[:, :]))
            own.wait()

            def rotate(dst, src, t, n, heads):
                half = ROPE // 2
                cos = const[0:n, C_ROPE + 64 * t:C_ROPE + 64 * t + 32]
                sin = const[0:n, C_ROPE + 64 * t + 32:C_ROPE + 64 * t + 64]
                a, b_ = ropet[0:n, 0, 0:heads, :], ropet[0:n, 1, 0:heads, :]

                def bc(z):
                    return z.unsqueeze(1).to_broadcast([n, heads, z.shape[1]])
                own.done(v.tensor_tensor(a, src, bc(cos), ALU.mult))
                own.done(v.tensor_tensor(b_[:, :, 0:half], src[:, :, half:ROPE], bc(sin[:, 0:half]), ALU.mult))
                own.done(v.tensor_tensor(b_[:, :, half:ROPE], src[:, :, 0:half], bc(sin[:, half:ROPE]), ALU.mult))
                own.wait()
                return v.tensor_tensor(dst, a, b_, ALU.add)

            for i, t in enumerate((2, 0, 1)):
                n = TILES[t][1]
                if i >= 1:
                    dve.wait_ge(lat_ready, i)
                v.scalar_tensor_tensor(out=lat[0:n, t, 0:QL], in0=PS[0:n, 2 * t, 0:QL],
                                       scalar=ri6[0:n, 2 * t:2 * t + 1], in1=gbc[0:n, B_GQL:B_GQL + QL],
                                       op0=ALU.mult, op1=ALU.mult)
                v.scalar_tensor_tensor(out=lat[0:n, t, QL:QL + KL], in0=PS[0:n, 2 * t + 1, 0:KL],
                                       scalar=ri6[0:n, 2 * t + 1:2 * t + 2], in1=gbc[0:n, B_GKL:B_GKL + KL],
                                       op0=ALU.mult, op1=ALU.mult)
                rotate(krope[0:n, t:t + 1, :], PS[0:n, 2 * t + 1, KL:KL + ROPE].unsqueeze(1), t, n, 1
                       ).then_inc(lat_ready, 1)
            dve.wait_ge(lat_ready, NT)
            own.done(v.tensor_copy(kvn[:, :], lat[0:NB, 2, QL:QL + KL]))

            with dve.Fori(0, 2) as i:
                for n in range(2):
                    j = 2 * i + n
                    for k in range(4):
                        ahead(Q_GLU + j, k)
                    b = 4 * ((G_GLU + n) % 2)
                    for m in range(2):
                        dve.wait_ge(sg_done, FT + 2 * j + m + 1)
                        i_ = v.tensor_tensor(zbuf[:, ds(2 * j + m, 1), CW - 1:CW - 1 + T].rearrange("p o n -> p (o n)"),
                                             sg[:, m, :], PS[:, b + m, 0:T], ALU.mult)
                        i_.then_inc(prod_done, 1)
                    dve.wait_ge(prod_done, FT + 2 * j + 4)
                    dve.sem_inc(g_free, 1)

            dve.wait_ge(latH_done, 2)
            for j in range(2):
                v.tensor_tensor(latL[:, 3 + j, :], PS[:, j, 0:T], latH[:, 3 + j, :].bitcast(F32), ALU.subtract
                                ).then_inc(latL_done, 1)
            own.done(v.tensor_copy(kvTn[:, :, :], PS[:, 0:2, SEQ:T]))
            dve.wait_ge(zst_done, 2)
            dve.wait_ge(latL_done, 2)
            own.wait()
            dve.sem_inc(use_dve, 1)
            dve.wait_ge(latH_done, 5)
            for j in range(3):
                v.tensor_tensor(latL[:, j, :], PS[:, 4 + j, 0:T], latH[:, j, :].bitcast(F32), ALU.subtract
                                ).then_inc(latL_done, 1)
            own.done(v.tensor_copy(krTn[:, :], PS[0:ROPE, 7, 0:NB]))
            dve.wait_ge(latL_done, 5)
            own.wait()
            dve.sem_inc(use_dve, 1)
            own.done(v.tensor_tensor(gqk[:, :], vecT[:, V_GQH:V_GQH + 1], vecT[:, V_GKH:V_GKH + 1], ALU.mult))
            own.done(v.tensor_tensor(gqkb[:, :], gbc[0:NB, B_GQH:B_GQH + QK], gbc[0:NB, B_GKH:B_GKH + QK], ALU.mult))
            own.wait()
            own.done(v.tensor_scalar(gqkb[:, :], gqkb[:, :], SCALE, None, ALU.mult))
            v.tensor_scalar(gqk[:, :], gqk[:, :], SCALE, None, ALU.mult).then_inc(rest_sb, 1)

            def head_norm(i, tok3, n, scale_tok=True):
                dve.wait_ge(tok_ss, i + 1)
                v.tensor_reduce(hss[0:n, i, :], junk[0:n, 0:H * QK].rearrange("p (h d) -> p h d", h=H),
                                AX_X, ALU.add).then_inc(tok_root, 1)
                dve.wait_ge(tok_root, 2 * i + 2)
                own.done(v.reciprocal(hrs[0:n, i, :], hss[0:n, i, :]))
                own.wait()
                if scale_tok:
                    return v.tensor_tensor(tok3, tok3, hrs[0:n, i, :].unsqueeze(2).to_broadcast([n, H, QK]), ALU.mult)

            for t in range(NT):
                n = TILES[t][1]
                dve.wait_ge(tok_ready, t + 1)
                own.done(v.tensor_copy(ktok[t][0:n, :, NOPE:QK], krope[0:n, t, :].unsqueeze(1).to_broadcast([n, H, ROPE])))
                own.wait()
                if t >= 1:
                    dve.sem_inc(use_dve, 1)
                dve.sem_inc(tok_sq, 1)
                i_ = head_norm(t, ktok[t][0:n, :, :], n, t < 2)
                if t < 2:
                    i_.then_inc(tok_done, 1)
            for n_ in range(6):
                ahead(Q_UQV + n_ // 4, n_ % 4)
            for n_ in range(2):
                ahead(Q_UQV + 1, 2 + n_)
            for n_ in range(7, 14):
                read(dve, n_)
            def samples_q():
                filled(dve, 14)
                own.done(v.tensor_copy(qnT[:, :, :], PS[:, 0, 0:64].rearrange("p (a b) -> p a b", b=NB)))
                own.done(v.tensor_copy(qrT[:, :, :], PS[:, 0, 64:192].rearrange("p (a b) -> p a b", b=NB)))
                own.wait()
                dve.sem_inc(rest_sb, 1)
                dve.wait_ge(memz, 5)
                for j in range(4):
                    a = slice(32 * j, 32 * j + 32)
                    own.done(v.tensor_copy(qbd[a, :, j, :].rearrange("p b h -> p h b"), qrT[a, :, :]))
                own.wait()
                dve.sem_inc(rest_sb, 1)

            for i, t in enumerate((2, 0, 1)):
                n = TILES[t][1]
                part = qtok[0:n, t, :, NOPE:QK]
                own.done(rotate(part, part, t, n, H))
                own.wait()
                dve.sem_inc(tok_sq, 1)
                i_ = head_norm(NT + i, qtok[0:n, t, :, :], n)
                if t < 2:
                    i_.then_inc(tok_done, 1)
                else:
                    own.done(i_)
                    own.wait()
                    own.done(v.tensor_tensor(qtok[0:n, t, :, :], qtok[0:n, t, :, :],
                                             gqkb[:, :].unsqueeze(1).to_broadcast([n, H, QK]), ALU.mult))
                    own.wait()
                    own.done(v.tensor_copy(qnrow[:, :, :], qtok[0:n, t, :, 0:NOPE]))
                    for r in range(4):
                        own.done(v.tensor_copy(qr4[:, :, r, :], qtok[0:n, t, :, NOPE:QK]))
                    own.wait()
                    dve.sem_inc(tok_done, 1)
                if t == 0:
                    samples_q()
            dve.wait_ge(qah_done, 1)
            v.tensor_tensor(qaL[:, :, :, :], qabs[:, :, :, :], qaH[:, :, :, :].bitcast(F32), ALU.subtract
                            ).then_inc(rest_sb, 1)
            filled(dve, 16)
            own.done(v.tensor_tensor(snew[:, :, :], PS[0:NB, 0, 0:128].rearrange("p (b h) -> p b h", b=NB),
                                     hrs[0:NB, 2, :].unsqueeze(1).to_broadcast([NB, NB, H]), ALU.mult))
            own.wait()
            dve.sem_inc(rest_sb, 1)
            own.done(v.tensor_tensor(snew[:, :, :], snew[:, :, :],
                                     const[0:NB, C_NEW:C_NEW + 128].rearrange("p (b h) -> p b h", b=NB), ALU.add))
            own.wait()

            def mask_max(hd):
                s = hd % 2
                dve.wait_ge(sc_ps, hd + 1)
                if hd >= 2:
                    dve.wait_ge(exp_done, hd - 1)
                v.tensor_tensor(sS[:, s, :], PS[:, s, 0:384], const[:, C_MASK:C_MASK + 384], ALU.add
                                ).then_inc(masked, 1)
                dve.wait_ge(masked, hd + 1)
                v.tensor_reduce(nm[:, s, 0:1], sS[:, s, 0:128], AX_X, ALU.max, negate=True)
                v.tensor_reduce(nm[:, s, 1:2], sS[:, s, 128:384], AX_X, ALU.max, negate=True).then_inc(nmax, 1)

            mask_max(0)
            for hd in range(H):
                s = hd % 2
                if hd + 1 < H:
                    mask_max(hd + 1)
                dve.wait_ge(exp_done, hd + 1)
                own.done(v.reciprocal(rl[:, s, :], ls[:, s, :]))
                own.wait()
                v.tensor_scalar(pS[:, s, 0:128], pS[:, s, 0:128], rl[:, s, 0:1], None, ALU.mult)
                v.tensor_scalar(pS[:, s, 128:384], pS[:, s, 128:384], rl[:, s, 1:2], None, ALU.mult
                                ).then_inc(pn_done, 1)
                if hd >= 2 and hd % 2 == 0:
                    dve.wait_ge(pv_ps, hd)
                    v.tensor_copy(oT[:, hd // 2 - 1, 0:SEQ], PS[:, 4 + (hd // 2 - 1) % 2, 0:SEQ]).then_inc(o_sb, 1)
            dve.wait_ge(pv_ps, H)
            v.tensor_copy(oT[:, H // 2 - 1, 0:SEQ], PS[:, 4 + (H // 2 - 1) % 2, 0:SEQ]).then_inc(o_sb, 1)

            def page_lo(pg, n, b, s, first):
                dve.wait_ge(kTH_done, pg + 1)
                if n % 4 == 1:
                    own.wait()
                    own.done(v.tensor_copy(Srope[:, s, n - 1:n + 3, :],
                                           PS[:, 0, 384:448].rearrange("p (j h) -> p j h", h=H)))
                if n == 6 and not first:
                    dve.wait_ge(den_ps, b)
                    denominators(b - 1)
                v.tensor_tensor(kTL[:, n % 2, :], PS[:, 0, 0:KL], kTH[:, n % 2, :].bitcast(F32), ALU.subtract
                                ).then_inc(kTL_done, 1)

            def page_sum(pg, n, s):
                dve.wait_ge(knsq_done, pg + 3)
                v.tensor_reduce(nsum[:, s, n, :], sqb[:, n % 2, :].rearrange("p (h d) -> p h d", h=H),
                                AX_X, ALU.add).then_inc(knsum_done, 1)

            def denominators(b):
                dve.wait_ge(ol_done, b + 1)
                own.done(v.reciprocal(rden[:, :], PS[0:H, 0, 448:449]))

            def put_q(b, s):
                for wq, qa in ((wqH, qaH), (wqL, qaL)):
                    c = (H + D) * s
                    i_ = v.tensor_copy(wq[:, :, c:c + H], qa[:, ds(b, 1), :, :].rearrange("p o k h -> p (o k) h"))
                i_.then_inc(qx_done, 1)

            def raw_scores(b, s):
                own.wait()
                dve.wait_ge(knsq_done, NPG * b + NPG + 2)
                own.done(v.tensor_tensor(S[:, s, 0:NPG, :], S[:, s, 0:NPG, :], Srope[:, s, :, :], ALU.add))

            def rope_squares(b, s):
                kr = kr2[:, s, :, :]
                own.wait()
                own.done(v.tensor_tensor(krq[:, :, :], kr, kr, ALU.mult))
                own.wait()
                own.done(v.tensor_reduce(ssr[:, s, :], krq[:, :, :], AX_X, ALU.add))

            def norm_sums(b, s):
                own.wait()
                dve.wait_ge(knsum_done, NPG * b + NPG + 2)
                ns = nsum[:, s, :, :]
                v.tensor_tensor(ns, ns, ssr[:, s, :].unsqueeze(2).to_broadcast([P, NPG, H]), ALU.add
                                ).then_inc(norm_sum, 1)

            def scores(b, s):
                dve.wait_ge(norm_root, b + 1)
                ns = nsum[:, s, :, :]
                own.done(v.reciprocal(ns, ns))
                own.done(v.tensor_copy(S[0:NB, s, NPG, :], snew[:, ds(b, 1), :].rearrange("p o h -> p (o h)")))
                own.wait()
                own.done(v.tensor_tensor(S[:, s, 0:NPG, :], S[:, s, 0:NPG, :], ns, ALU.mult))
                own.wait()
                v.tensor_reduce(mx[:, s, :], S[:, s, :, :].rearrange("p j h -> p h j"), AX_X, ALU.max
                                ).then_inc(mx_done, 1)

            def subtract(b, s):
                dve.wait_ge(gmx_done, b + 1)
                sv = S[:, s, :, :]
                v.tensor_tensor(sv, sv, gmx[:, s, :].unsqueeze(1).to_broadcast([P, NPG + 1, H]), ALU.subtract
                                ).then_inc(sub_done, 1)

            def sums(b, s):
                dve.wait_ge(p_done, b + 3)
                v.tensor_reduce(lsum[:, s, :], Pr[:, s, :, :].rearrange("p j h -> p h j"), AX_X, ALU.add
                                ).then_inc(lsum_done, 1)

            def latent_out(b):
                dve.wait_ge(pg_rel, 4 * b + 12)
                own.wait()
                v.tensor_scalar(olrow[:, ds(b, 1), :].rearrange("p o n -> p (o n)"), PS[0:H, 1, 0:KL], rden[:, :], None,
                                ALU.mult).then_inc(ol_done, 1)

            def tap(f_, t):
                y = u[:, ds(f_, 1), 0:SEQ].rearrange("p o n -> p (o n)")
                z = zbuf[:, ds(f_, 1), t:t + SEQ].rearrange("p o n -> p (o n)")
                w = wdw[:, ds(f_, 1), t:t + 1].rearrange("p o n -> p (o n)")
                own.wait()
                if t == 0:
                    own.done(v.tensor_scalar(y, z, w, vecT[:, ds(V_BDW + f_, 1)], ALU.mult, ALU.add))
                else:
                    own.done(v.scalar_tensor_tensor(out=y, in0=z, scalar=w, in1=y, op0=ALU.mult, op1=ALU.add))

            def sequence(b, s, first=False, last=False):
                for n in range(NPG):
                    pg = NPG * b + n
                    if not (last and n == NPG - 1):
                        page_lo(pg + 1, (n + 1) % NPG, b, s, first)
                    tap(b, 2 * n)
                    if n > 0:
                        page_sum(pg - 1, n - 1, s)
                    elif not first:
                        page_sum(pg - 1, NPG - 1, 1 - s)
                    if not first:
                        if n == 0:
                            raw_scores(b - 1, 1 - s)
                            norm_sums(b - 1, 1 - s)
                        if n == 1:
                            scores(b - 1, 1 - s)
                        if n == 2:
                            subtract(b - 1, 1 - s)
                        if n == 3:
                            sums(b - 1, 1 - s)
                        if n == 12:
                            latent_out(b - 1)
                    if 2 * n + 1 < CW:
                        tap(b, 2 * n + 1)
                    if n == 5 and not last:
                        put_q(b + 1, 1 - s)
                    if n == 13:
                        rope_squares(b, s)

            dve.sem_inc(p_done, 2)
            dve.sem_inc(ol_done, 1)
            dve.wait_ge(memz, 6)
            dve.wait_ge(rest_sb, 5)
            put_q(0, 0)
            page_lo(0, 0, 0, 0, True)
            sequence(0, 0, first=True)
            with dve.Fori(0, 3) as i:
                own.loop(i, 2 * (CW + 11))
                sequence(2 * i + 1, 1)
                sequence(2 * i + 2, 0)
                own.end(3)
            sequence(7, 1, last=True)
            page_sum(PAGES - 1, NPG - 1, 1)
            raw_scores(7, 1)
            norm_sums(7, 1)
            scores(7, 1)
            subtract(7, 1)
            sums(7, 1)
            dve.wait_ge(den_ps, NB)
            denominators(7)
            latent_out(7)

            ys = u[:, :, SEQ:T]
            dve.wait_ge(pg_rel, 4 * NB + 8)
            own.done(v.tensor_tensor(dtmp[:, :, :, :], stbuf[:, :, :, :],
                                     wdw[:, :, 0:CW - 1].unsqueeze(2).to_broadcast([P, KT, NB, CW - 1]), ALU.mult))
            own.wait()
            own.done(v.tensor_reduce(ys, dtmp[:, :, :, :], AX_X, ALU.add))
            zn = dtmp[:, 0, :, 0:KT].rearrange("p b f -> p f b")
            own.wait()
            own.done(v.tensor_tensor(zn, zbuf[:, :, CW - 1 + SEQ:CW - 1 + T],
                                     wdw[:, :, CW - 1:CW].to_broadcast([P, KT, NB]), ALU.mult))
            own.wait()
            own.done(v.tensor_tensor(ys, ys, zn, ALU.add))
            own.wait()
            v.tensor_tensor(ys, ys, vecT[:, V_BDW:V_BDW + KT].unsqueeze(2).to_broadcast([P, KT, NB]), ALU.add
                            ).then_inc(y_done, 1)
            dve.wait_ge(y_done, 1)
            dve.sem_inc(z_free, 1)

            dve.wait_ge(mean_ps, 1)
            for kt in range(KT):
                v.scalar_tensor_tensor(out=u[:, kt, :], in0=PS[:, 2, 0:T], scalar=-1.0 / D, in1=u[:, kt, :],
                                       op0=ALU.mult, op1=ALU.add).then_inc(yc_done, 1)
            for kt in range(KT):
                dve.wait_ge(oh_done, kt + 1)
                v.tensor_tensor(oL[:, kt, :], oT[:, kt, :], oH[:, kt, :].bitcast(F32), ALU.subtract
                                ).then_inc(ol2_done, 1)
            with dve.Fori(0, 2) as j:
                for k in range(4):
                    ahead(Q_GATE + j, k)
            dve.wait_ge(ysd_done, 1)
            own.done(v.reciprocal(rinv[:, :], rs[:, :]))
            own.wait()
            for kt in range(KT):
                v.tensor_tensor(u[:, kt, :], u[:, kt, :], rinv[:, :], ALU.mult).then_inc(yn_done, 1)
            with dve.Fori(2, 4) as j:
                for k in range(4):
                    ahead(Q_GATE + j, k)
            for kt in range(KT):
                dve.wait_ge(yh_done, kt + 1)
                v.tensor_tensor(yL[:, kt, :], u[:, kt, :], yH[:, kt, :].bitcast(F32), ALU.subtract
                                ).then_inc(yl_done, 1)
            dve.wait_ge(g_free, G_AO + 2)
            with dve.Fori(0, 2) as j:
                for m in range(2):
                    for k in range(2):
                        ahead(Q_AO + j, 2 * m + k)
                    dve.wait_ge(w_used, 4 * (Q_AO + j) + 2 * m + 2)
                    b = 4 * ((G_AO + m) % 2)
                    t = ds(4 * j + 2 * m, 2)
                    v.tensor_tensor(mrg[:, t, :], sig[:, t, :], PS[:, b:b + 2, 0:T], ALU.mult).then_inc(g_free, 1)
            with dve.Fori(0, 2) as j:
                own.loop(j, 2)
                for m in range(2):
                    for k in range(2):
                        ahead(Q_CO + j, 2 * m + k)
                    dve.wait_ge(w_used, 4 * (Q_CO + j) + 2 * m + 2)
                    b = 4 * ((G_CO + m) % 2)
                    t = ds(4 * j + 2 * m, 2)
                    own.done(v.tensor_tensor(ctmp[:, :, :], sig[:, ds(KT + 4 * j + 2 * m, 2), :], PS[:, b:b + 2, 0:T],
                                             ALU.mult))
                    own.wait()
                    v.tensor_tensor(mrg[:, t, :], mrg[:, t, :], ctmp[:, :, :], ALU.add).then_inc(mrg_done, 1)
                    dve.wait_ge(mh_done, 2 * j + m + 1)
                    v.tensor_tensor(uL[:, t, :], mrg[:, t, :], uH[:, t, :].bitcast(F32), ALU.subtract
                                    ).then_inc(g_free, 1)
                own.end(2)
            with dve.Fori(0, 2) as j:
                own.loop(j, 2)
                for m in range(2):
                    for k in range(2):
                        ahead(Q_WO + j, 2 * m + k)
                    dve.wait_ge(w_used, 4 * (Q_WO + j) + 2 * m + 2)
                    residual(4 * j + 2 * m, 4 * ((G_WO + m) % 2), KT * GM, G_WO + 2 * j + m)
                own.end(2)
            prenorm(2)
            ffn_in(Q_FFN2_IN, G_FFN2_IN, FT + KT, FT)
            ffn_out(Q_FFN2_OUT, G_FFN2_OUT, GF2, True)

        @block.tensor
        def _(pe):
            mm = nc.tensor.matmul
            tr = nc.tensor.transpose

            def product(dst, a, b, start, stop):
                mm(dst, a[0], b[0], start=start, stop=False)
                mm(dst, a[0], b[1], start=False, stop=False)
                return mm(dst, a[1], b[0], start=False, stop=stop)

            def pair(q, ks, kts, banks, mov, nk, norm=None):
                for i, (dq, k) in enumerate(ks):
                    pe.wait_ge(w_lo, 4 * (q + dq) + k + 1)
                    k0, k1 = kts[i]
                    for m in range(2):
                        for kt in range(k0, k1):
                            if norm is not None and m == 0:
                                pe.wait_ge(u_ready, (KT + 1) * norm + kt + 2)
                            c = slice((kt - k0) * 256 + 128 * m, (kt - k0) * 256 + 128 * m + 128)
                            i_ = product(PS[:, banks + m, 0:mov[0].shape[2]], (wH[:, k, c], wL[:, k, c]),
                                         (mov[0][:, kt, :], mov[1][:, kt, :]), kt == 0, kt == nk - 1)
                    i_.then_inc(w_used, 1)

            pe.wait_ge(memz, 4)
            pe.wait_ge(in_vec, 16 * 13)
            for kt in range(KT):
                tr(PS[:, 0, NS * kt:NS * kt + NS], crow[:, P * kt:P * kt + P], ident[0:NS, 0:NS])
            tr(PS[:, 0, 72:72 + V_N], vrow[0:V_N, :], ident[0:V_N, 0:V_N])
            for kt in range(KT):
                i_ = tr(PS[:, 0, 200 + CW * kt:200 + CW * kt + CW], dwrow[:, P * kt:P * kt + P], ident[0:CW, 0:CW])
            i_.then_inc(vec_ps, 1)
            pe.sem_inc(at_ps, 2)
            pe.wait_ge(vec_sb, 1)
            pe.wait_ge(cs_lo, 1)

            def mod_rows(j, m):
                pe.wait_ge(arow_done, 2 * j + m + 1)
                for i in range(2):
                    k = 2 * m + i
                    pe.wait_ge(w_lo, 4 * (Q_ADA + j) + k + 1)
                    for kt in range(4):
                        c = slice(256 * kt, 256 * kt + 256)
                        i_ = product(PS[0:NS + 1, 4 * m, 0:256], (csH[:, 4 * i + kt, :], csL[:, 4 * i + kt, :]),
                                     (wH[:, k, c], wL[:, k, c]), (i, kt) == (0, 0), (i, kt) == (1, 3))
                    i_.then_inc(w_used, 1)

            def mod_turned(j, m):
                pe.wait_ge(arow_done, 2 * j + m + 3)
                pe.wait_ge(g_free, G_ADA + 2 * j + m + 1)
                for n in range(2):
                    i_ = tr(PS[:, 1 + 4 * m, P * n:P * n + P], arow[:, m, P * n:P * n + P], ident)
                i_.then_inc(at_ps, 1)

            mod_rows(0, 0)
            with pe.Fori(0, 17) as j:
                mod_rows(j, 1)
                mod_turned(j, 0)
                mod_rows(j + 1, 0)
                mod_turned(j, 1)
            mod_rows(17, 1)
            mod_turned(17, 0)
            mod_turned(17, 1)
            pe.wait_ge(g_free, G_FFN1_IN + 2)
            pe.wait_ge(in_gain, 80)
            mm(PS[:, 1, :], ones[0:1, :], grow[0:1, 0:512], start=True, stop=True)
            mm(PS[:, 2, 0:B_N - 512], ones[0:1, :], grow[0:1, 512:B_N], start=True, stop=True).then_inc(gain_ps, 1)
            pe.wait_ge(in_x, 32)
            for kt in range(KT):
                if kt >= 4:
                    pe.wait_ge(x_sb, kt - 3)
                c = slice(P * kt, P * kt + P)
                for t in range(2):
                    tr(PS[:, 4 + kt % 4, 128 * t:128 * t + 128], xrow[:, t, c], ident)
                tr(PS[:, 4 + kt % 4, SEQ:T], xsrow[:, c], ident[0:NB, 0:NB]).then_inc(x_ps, 1)
            pe.wait_ge(in_st, 32)
            pe.wait_ge(x_sb, KT)
            for i in range(2):
                for kt in range(KT):
                    i_ = tr(PS[:, 4 + 2 * i + kt // 4, 120 * (kt % 4):120 * (kt % 4) + 120],
                            strow[:, i, P * kt:P * kt + P], ident[0:120, 0:120])
            i_.then_inc(st_ps, 1)
            pe.wait_ge(gain_sb, 1)

            def prenorm(n):
                for kt in range(KT):
                    pe.wait_ge(sq_done, KT * n + kt + 1)
                    i_ = mm(PS[:, 2, 0:T], ones[:, :], u[:, kt, :], start=(kt == 0), stop=(kt == KT - 1))
                i_.then_inc(ssq_ps, 1)

            def ffn_in(q0, g0, norm):
                ks = [(0, k) for k in range(2)], [(0, k) for k in range(2, 4)]
                kts = [(0, 4), (4, 8)]

                def go(j, b, norm=None):
                    pe.wait_ge(g_free, g0 + j + 1)
                    pair(q0 + j, ks[0], kts, b, (uH, uL), KT, norm)
                    pair(q0 + j, ks[1], kts, b + 2, (uH, uL), KT)

                go(0, 4 * (g0 % 2), norm)
                with pe.Fori(0, 5) as i:
                    for n in range(2):
                        go(2 * i + 1 + n, 4 * ((g0 + 1 + n) % 2))

            def ffn_out(q0, g0):
                pe.wait_ge(g_free, g0 + 2)
                with pe.Fori(0, 2) as i:
                    for n in range(2):
                        pe.wait_ge(g_free, g0 + 2 * i + n + 1)
                        ks = [((6 * n + c) // 4, (6 * n + c) % 4) for c in range(6)]
                        pair(q0 + 3 * i, ks, OUT_KTS, 4 * ((g0 + n) % 2), (aH, aL), FT)

            def pairs(q0, g0, mov, lo_, hi_):
                with pe.Fori(lo_, hi_) as j:
                    for m in range(2):
                        pe.wait_ge(g_free, g0 + 2 * j + m + 1)
                        pair(q0 + j, [(0, 2 * m), (0, 2 * m + 1)], [(0, 4), (4, 8)], 4 * ((g0 + m) % 2), mov, KT)

            prenorm(0)
            pe.wait_ge(st_sb, 4)
            ffn_in(Q_FFN1_IN, G_FFN1_IN, 0)
            ffn_out(Q_FFN1_OUT, G_FFN1_OUT)
            prenorm(1)

            for kt in range(KT):
                q, k = Q_QKV + kt // 4, kt % 4
                pe.wait_ge(w_lo, 4 * q + k + 1)
                pe.wait_ge(u_ready, KT + 1 + kt + 2)
                for t, (t0, n) in enumerate(TILES):
                    a = (uH[:, kt, t0:t0 + n], uL[:, kt, t0:t0 + n])
                    product(PS[0:n, 2 * t, 0:QL], a, (wH[:, k, 0:QL], wL[:, k, 0:QL]), kt == 0, kt == KT - 1)
                    i_ = product(PS[0:n, 2 * t + 1, 0:LAT - QL], a, (wH[:, k, QL:LAT], wL[:, k, QL:LAT]),
                                 kt == 0, kt == KT - 1)
                i_.then_inc(w_used, 1)

            def glu(j, b):
                pe.wait_ge(g_free, G_GLU + j + 1)
                pair(Q_GLU + j, [(0, 0), (0, 1)], [(0, 4), (4, 8)], b, (uH, uL), KT)
                pair(Q_GLU + j, [(0, 2), (0, 3)], [(0, 4), (4, 8)], b + 2, (uH, uL), KT)

            pe.wait_ge(lat_ready, NT)
            with pe.Fori(0, 2) as i:
                for n in range(2):
                    glu(2 * i + n, 4 * ((G_GLU + n) % 2))
            pe.wait_ge(g_free, G_GATE + 2)

            for j in range(2):
                for t, (t0, n) in enumerate(TILES):
                    tr(PS[:, j, t0:t0 + n], lat[0:n, t, QL + 128 * j:QL + 128 * j + 128], ident[0:n, 0:n])
            for kt in range(KT):
                i_ = tr(PS[0:CW - 1 + NB, 2 + kt // 4, 128 * (kt % 4):128 * (kt % 4) + 128],
                        zbuf[:, kt, SEQ:CW - 1 + T], ident)
            i_.then_inc(use_ps, 1)
            for j in range(3):
                for t, (t0, n) in enumerate(TILES):
                    tr(PS[:, 4 + j, t0:t0 + n], lat[0:n, t, 128 * j:128 * j + 128], ident[0:n, 0:n])
            tr(PS[0:ROPE, 7, 0:NB], krope[0:NB, 2, :], ident[0:NB, 0:NB]).then_inc(use_ps, 1)
            for t, (t0, n) in enumerate(TILES):
                if t == 0:
                    pe.wait_ge(wukl_done, 1)
                    pe.wait_ge(latL_done, 2)
                    read(pe, 0)
                if t == 2:
                    read(pe, 1)
                for c in range(2):
                    for kt in range(2):
                        i_ = product(PS[0:n, 2 * t + c, :],
                                     (latH[:, 3 + kt, t0:t0 + n], latL[:, 3 + kt, t0:t0 + n]),
                                     (wukH[:, kt, 512 * c:512 * c + 512], wukL[:, kt, 512 * c:512 * c + 512]),
                                     kt == 0, kt == 1)
                if t >= 1:
                    i_.then_inc(use_ps, 1)
            read(pe, 2)
            for j in range(H // 2):
                for kt in range(2):
                    at = KL * j + 128 * kt
                    i_ = tr(PS[:, at // 512, at % 512:at % 512 + 128], wukF[:, kt, 128 * j:128 * j + 128], ident)
            i_.then_inc(use_ps, 1)

            def by_head(use, tok):
                b = 4 * (use % 2)
                for hd in range(H):
                    i_ = tr(PS[0:QK, b + hd // 4, 128 * (hd % 4):128 * (hd % 4) + 128], tok[:, hd, :], ident)
                i_.then_inc(use_ps, 1)

            for t in range(2):
                read(pe, 3 + t)
                pe.wait_ge(tok_done, t + 1)
                by_head(5 + t, ktok[t])
            pe.wait_ge(latL_done, 5)
            for n_ in range(6):
                q, k = Q_UQV + n_ // 4, n_ % 4
                read(pe, 5 + n_)
                pe.wait_ge(w_lo, 4 * q + k + 1)
                b = 4 * ((7 + n_) % 2)
                for t, (t0, n) in enumerate(TILES):
                    for kt in range(3):
                        i_ = product(PS[0:n, b + t, 0:256], (latH[:, kt, t0:t0 + n], latL[:, kt, t0:t0 + n]),
                                     (wH[:, k, 256 * kt:256 * kt + 256], wL[:, k, 256 * kt:256 * kt + 256]),
                                     kt == 0, kt == 2)
                i_.then_inc(w_used, 1)
            read(pe, 11)
            for n_ in range(2):
                pe.wait_ge(w_lo, 4 * (Q_UQV + 1) + 2 + n_ + 1)
                for t in range(2):
                    for kt in range(2):
                        c = slice(512 * kt, 512 * kt + 512)
                        i_ = product(PS[:, 4 + 2 * n_ + t, :],
                                     (latH[:, 3 + kt, 128 * t:128 * t + 128], latL[:, 3 + kt, 128 * t:128 * t + 128]),
                                     (wH[:, 2 + n_, c], wL[:, 2 + n_, c]), kt == 0, kt == 1)
                i_.then_inc(w_used, 1)
            read(pe, 12)
            pe.wait_ge(tok_done, 3)
            for j in range(H // 2):
                tr(PS[:, 0, NB * j:NB * j + NB], qnrow[:, 2 * j:2 * j + 2, :].rearrange("p a d -> p (a d)"), ident[0:NB, 0:NB])
            for hd in range(H):
                i_ = tr(PS[:, 0, 64 + NB * hd:64 + NB * hd + NB],
                        qr4[:, hd, :, :].rearrange("p r d -> p (r d)"), ident[0:NB, 0:NB])
            i_.then_inc(use_ps, 1)
            read(pe, 13)
            pe.wait_ge(rest_sb, 2)
            read(pe, 4)
            for kt in range(2):
                for hd in range(H):
                    a = slice(64 * (hd % 2), 64 * (hd % 2) + 64)
                    at = 64 * kt + NB * (hd // 2)
                    i_ = mm(PS[:, 4 + hd % 2, at:at + NB], wukT[a, hd // 2, 128 * kt:128 * kt + 128], qnT[a, hd // 2, :],
                            start=True, stop=True)
            i_.then_inc(use_ps, 1)
            read(pe, 15)
            for kt in range(2):
                mm(PS[0:NB, 0, 0:128], kvTn[:, kt, :], qabs[:, :, kt, :], start=(kt == 0), stop=False)
            mm(PS[0:NB, 0, 0:128], krTn[:, :], qrT[0:ROPE, :, :].rearrange("p h b -> p b h"), start=False, stop=True
               ).then_inc(use_ps, 1)
            for t in range(2):
                if t == 1:
                    pe.wait_ge(rest_sb, 5)
                pe.wait_ge(tok_done, 4 + t)
                by_head(17 + t, qtok[:, t, :, :])
            read(pe, 18)

            def scores(hd):
                b = hd % 2
                if hd >= 2:
                    pe.wait_ge(masked, hd - 1)
                mm(PS[:, b, 0:128], qT[:, hd, 0:128], kT[:, hd, 0:128], start=True, stop=True)
                mm(PS[:, b, 128:384], qT[:, hd, 128:256], kT[:, hd, :], start=True, stop=True).then_inc(sc_ps, 1)

            def turn_probs(hd):
                b = 2 + hd % 2
                pe.wait_ge(pn_done, hd + 1)
                if hd >= 2:
                    pe.wait_ge(pT_sb, hd - 1)
                for j in range(3):
                    c = slice(128 * j, 128 * j + 128)
                    i_ = tr(PS[:, b, c], pS[:, hd % 2, c], ident)
                i_.then_inc(pT_ps, 1)

            def values(hd):
                b = 4 + (hd // 2) % 2
                a = slice(64 * (hd % 2), 64 * (hd % 2) + 64)
                vc = slice(VH * hd, VH * hd + VH)
                pe.wait_ge(pT_sb, hd + 1)
                if hd % 2 == 0 and hd >= 4:
                    pe.wait_ge(o_sb, hd // 2 - 1)
                mm(PS[a, b, 0:SEQ], vtok[:, 0, vc], pTs[:, hd % 2, 0:SEQ], start=True, stop=False)
                mm(PS[a, b, 128:SEQ], vtok[:, 1, vc], pTs[:, hd % 2, SEQ:384], start=False, stop=True
                   ).then_inc(pv_ps, 1)

            pe.sem_inc(kn_ps, 2)
            pe.sem_inc(pg_rel, 8)
            scores(0)
            scores(1)
            for hd in range(H):
                if hd + 2 < H:
                    scores(hd + 2)
                turn_probs(hd)
                if hd >= 1:
                    values(hd - 1)
            values(H - 1)

            def denominator(b, s):
                pe.wait_ge(lsum_done, b + 1)
                mm(PS[0:H, 0, 448:450], lsum[:, s, :], ones[:, 0:2], start=True, stop=True).then_inc(den_ps, 1)

            def turn(use, s, n, pg, b, first):
                if n % 4 == 0:
                    pe.wait_ge(kv2_in[4 * s + n // 4], 128 * use + 128)
                pe.wait_ge(kTL_done, pg + 2)
                if n % 4 == 0:
                    tr(PS[:, 0, KL:KL + P], kr2[:, s, n:n + 4, :].rearrange("p a b -> p (a b)"), ident)
                if n % 4 == 1:
                    mm(PS[:, 0, 384:448], krT[:, (n // 4) % 2, :],
                       qbd[:, ds(b, 1), :, :].rearrange("p o j h -> p (o j h)"), start=True, stop=True)
                if n == 6 and not first:
                    denominator(b - 1, 1 - s)
                tr(PS[:, 0, 0:128], kv2[:, NPG * s + n, 0:128], ident)
                tr(PS[:, 0, 128:256], kv2[:, NPG * s + n, 128:256], ident).then_inc(kT_ps, 1)

            def keys(b, sq, n, pg):
                s = n % 2
                pe.wait_ge(kTL_done, pg + 3)
                pe.wait_ge(knsq_done, pg + 1)
                if n == 0:
                    pe.wait_ge(qx_done, b + 1)
                for c0, c1, bank, at in KEYS[sq]:
                    for kt in range(2):
                        a = slice(128 * kt, 128 * kt + 128)
                        i_ = product(PS[:, 2 + 3 * s + bank, at:at + c1 - c0], (kTH[:, s, a], kTL[:, s, a]),
                                     (wqH[:, kt, c0:c1], wqL[:, kt, c0:c1]), kt == 0, kt == 1)
                i_.then_inc(kn_ps, 1)

            def page_values(b, s, n):
                if n == 0:
                    pe.wait_ge(ol_done, b + 1)
                    pe.wait_ge(p_done, b + 3)
                i_ = mm(PS[0:H, 1, 0:KL], Pr[:, s, n, :], kv2[:, NPG * s + n, :], start=(n == 0), stop=(n == NPG - 1))
                if n == 0:
                    mm(PS[0:H, 1, 0:KL], Pr[0:NB, s, NPG, :], kvn[:, :], start=False, stop=False)
                if n % 4 == 3:
                    i_.then_inc(pg_rel, 1)

            def sequence(b, s, use, first=False, last=False):
                for n in range(NPG):
                    pg = NPG * b + n
                    if n + 1 < NPG:
                        turn(use, s, n + 1, pg + 1, b, first)
                    elif not last:
                        turn(use + s, 1 - s, 0, pg + 1, b + 1, False)
                    keys(b, s, n, pg)
                    if not first and 4 <= n < 12:
                        for m in range(2):
                            page_values(b - 1, 1 - s, 2 * (n - 4) + m)

            pe.wait_ge(o_sb, H // 2)
            turn(0, 0, 0, 0, 0, True)
            sequence(0, 0, 0, first=True)
            with pe.Fori(0, 3) as i:
                sequence(2 * i + 1, 1, i)
                sequence(2 * i + 2, 0, i + 1)
            sequence(7, 1, 3, last=True)
            denominator(7, 1)
            for n in range(NPG):
                page_values(7, 1, n)
            pe.wait_ge(ol_done, NB + 1)
            for kt in range(2):
                for b in range(NB):
                    i_ = tr(PS[:, 0, 128 * kt + H * b:128 * kt + H * b + H], olrow[:, b, 128 * kt:128 * kt + 128],
                            ident[0:H, 0:H])
            i_.then_inc(use_ps, 1)
            pe.wait_ge(os_sb, 1)
            pe.wait_ge(in_wuv, 16)
            for hd in range(H):
                a = slice(64 * (hd % 2), 64 * (hd % 2) + 64)
                for kt in range(2):
                    i_ = mm(PS[a, 1, NB * (hd // 2):NB * (hd // 2) + NB], wuvF[:, kt, VH * hd:VH * hd + VH],
                            olat[:, kt, hd, :], start=(kt == 0), stop=(kt == 1))
            i_.then_inc(os_ps, 1)

            pe.wait_ge(os_sb, 2)
            pe.wait_ge(y_done, 1)
            for kt in range(KT):
                i_ = mm(PS[:, 2, 0:T], ones[:, :], u[:, kt, :], start=(kt == 0), stop=(kt == KT - 1))
            i_.then_inc(mean_ps, 1)
            pairs(Q_GATE, G_GATE, (uH, uL), 0, 2)
            for kt in range(KT):
                pe.wait_ge(ysq_done, kt + 1)
                i_ = mm(PS[:, 3, 0:T], ones[:, :], mrg[:, kt, :], start=(kt == 0), stop=(kt == KT - 1))
            i_.then_inc(var_ps, 1)
            pairs(Q_GATE, G_GATE, (uH, uL), 2, 4)
            pe.wait_ge(ol2_done, KT)
            pairs(Q_AO, G_AO, (oH, oL), 0, 2)
            pe.wait_ge(yl_done, KT)
            pairs(Q_CO, G_CO, (yH, yL), 0, 2)
            pe.wait_ge(g_free, G_WO + 2)
            pairs(Q_WO, G_WO, (uH, uL), 0, 2)
            prenorm(2)
            ffn_in(Q_FFN2_IN, G_FFN2_IN, 2)
            ffn_out(Q_FFN2_OUT, G_FFN2_OUT)
            pe.wait_ge(g_free, G_END + 2)
            for t, (t0, n) in enumerate(TILES):
                for kt in range(KT):
                    i_ = tr(PS[0:n, 2 * t + kt // 4, 128 * (kt % 4):128 * (kt % 4) + 128], h[:, kt, t0:t0 + n], ident)
                i_.then_inc(fin_ps, 1)


INPUTS = ["x_prompt", "x_sample", "c_prompt", "c_sample", "cache_kv_latent", "cache_k_rope", "state_conv",
          "page_table", "w_ada", "b_ada", "g_norm_ffn1", "w_ffn1_in", "w_ffn1_out", "g_norm_mix", "w_in",
          "g_q_lat", "w_uq", "g_q_head", "g_kv_lat", "w_uk", "w_uv", "g_k_head", "w_attn_out", "w_dw", "b_dw",
          "g_conv_norm", "b_conv_norm", "w_conv_out", "w_out", "g_norm_ffn2", "w_ffn2_in", "w_ffn2_out"]
OUTPUTS = [("y_prompt", (1, SEQ, D)), ("y_sample", (NB, 1, D)), ("kv_latent_prompt", (1, SEQ, KL)),
           ("k_rope_prompt", (1, SEQ, ROPE)), ("conv_state_prompt", (1, CW - 1, D)),
           ("kv_latent_sample", (NB, 1, KL)), ("k_rope_sample", (NB, 1, ROPE)),
           ("conv_state_sample", (NB, CW - 1, D))]


def kernel(**inputs):
    import concourse.bacc as bacc
    from concourse.bass_utils import run_bass_kernel_spmd

    nc = bacc.Bacc("TRN2", target_bir_lowering=False, num_devices=1, dynamic_dma_scratch_size=1024)
    arrays = {name: np.ascontiguousarray(inputs[name]) for name in INPUTS}
    arrays["const"] = constants()
    x = {name: nc.dram_tensor(f"in_{name}", a.shape, mybir.dt.from_np(a.dtype), kind="ExternalInput").ap()
         for name, a in arrays.items()}
    out = {name: nc.dram_tensor(f"out_{name}", shape, F32, kind="ExternalOutput").ap() for name, shape in OUTPUTS}
    decoder_layer(nc, x, out)
    r = run_bass_kernel_spmd(nc, [{f"in_{name}": a for name, a in arrays.items()}], core_ids=[0])
    return tuple(r.results[0][f"out_{name}"] for name, _ in OUTPUTS)
```
